# Optimizing a Trainium2 kernel written in Bass

```python
import math
import jax, jax.numpy as jnp
from jax import lax
import numpy as np

D_MODEL = 1024
BATCH = 1
SEQ = 256
DEPTH = 1

CHUNK = 64
D_MIX = D_MODEL
GM_GROUPS = 8
GM_GROUP_DIM = 64
GM_WIDTH = GM_GROUPS * GM_GROUP_DIM
GM_BLOCK = 128
DN_HEADS = 4
DN_HEAD_DIM = 128
DN_WIDTH = DN_HEADS * DN_HEAD_DIM
DN_CONV = 4
D_IN = 2 * GM_WIDTH + 4 * DN_WIDTH + 2 * DN_HEADS
D_FF = 2816
EPS = 1e-6


def rmsnorm(x, g):
    xf = x.astype(jnp.float32)
    y = xf * lax.rsqrt(jnp.mean(xf * xf, axis=-1, keepdims=True) + EPS)
    return (y * g.astype(jnp.float32)).astype(x.dtype)

def layernorm(x, g, b):
    xf = x.astype(jnp.float32)
    mu = jnp.mean(xf, axis=-1, keepdims=True)
    var = jnp.mean(jnp.square(xf - mu), axis=-1, keepdims=True)
    y = (xf - mu) * lax.rsqrt(var + EPS)
    return (y * g.astype(jnp.float32) + b.astype(jnp.float32)).astype(x.dtype)

def l2norm(x):
    return x * lax.rsqrt(jnp.sum(x * x, axis=-1, keepdims=True) + EPS)

def swiglu(x, w_gate, w_up, w_down):
    return (jax.nn.silu(x @ w_gate) * (x @ w_up)) @ w_down

def chunk_causal_mask(n):
    c = jnp.arange(n) // CHUNK
    return c[None, :] <= c[:, None]

def spatial_gating(u, v, w_s, b_s, ln_g, ln_b):
    B, T, _ = v.shape
    v = layernorm(v, ln_g, ln_b)
    nb = T // GM_BLOCK
    vb = v.reshape(B, nb, GM_BLOCK, GM_GROUPS, GM_GROUP_DIM)
    w = jnp.where(chunk_causal_mask(GM_BLOCK)[None], w_s, 0.0).astype(v.dtype)
    mixed = jnp.einsum('gij,bnjgc->bnigc', w, vb) + b_s.T[:, :, None].astype(v.dtype)
    return u * mixed.reshape(B, T, GM_WIDTH)

def causal_dwconv(x, w):
    K, C = w.shape
    return lax.conv_general_dilated(
        x, w[:, None, :].astype(x.dtype), window_strides=(1,), padding=[(K - 1, 0)],
        dimension_numbers=('NWC', 'WIO', 'NWC'), feature_group_count=C)

def gated_delta_rule(q, k, v, beta, g):
    B, T, H, Dk = q.shape
    Dv = v.shape[-1]
    C = CHUNK
    N = T // C
    scale = Dk ** -0.5

    def to_chunks(t):
        return t.reshape(B, N, C, H, *t.shape[3:]).swapaxes(2, 3)

    q, k, v = to_chunks(q * scale), to_chunks(k), to_chunks(v)
    beta, g = to_chunks(beta), to_chunks(g)
    g = jnp.cumsum(g, axis=-1)
    tri = jnp.tril(jnp.ones((C, C), bool))
    strict = jnp.tril(jnp.ones((C, C), bool), -1)
    decay = jnp.exp(jnp.where(tri, g[..., :, None] - g[..., None, :], -jnp.inf))
    k_beta = k * beta[..., None]
    v_beta = v * beta[..., None]
    L = jnp.where(strict, jnp.einsum('bnhid,bnhjd->bnhij', k_beta, k) * decay, 0.0)
    eye = jnp.eye(C, dtype=L.dtype)
    rhs = jnp.concatenate([v_beta, k_beta * jnp.exp(g)[..., None]], axis=-1)
    sol = lax.linalg.triangular_solve(L + eye, rhs, left_side=True, lower=True,
                                      unit_diagonal=True)
    u_c, w_c = sol[..., :Dv], sol[..., Dv:]
    attn = jnp.where(tri, jnp.einsum('bnhid,bnhjd->bnhij', q, k) * decay, 0.0)
    g_last = g[..., -1]
    k_dec = k * jnp.exp(g_last[..., None] - g)[..., None]
    q_dec = q * jnp.exp(g)[..., None]
    xs = tuple(jnp.moveaxis(t, 1, 0) for t in (q_dec, k_dec, u_c, w_c, attn, g_last))

    def step(S, inp):
        qd, kd, uc, wc, a, gl = inp
        v_new = uc - jnp.einsum('bhcd,bhde->bhce', wc, S)
        o = jnp.einsum('bhcd,bhde->bhce', qd, S) + jnp.einsum('bhij,bhje->bhie', a, v_new)
        S = S * jnp.exp(gl)[..., None, None] + jnp.einsum('bhcd,bhce->bhde', kd, v_new)
        return S, o

    S0 = jnp.zeros((B, H, Dk, Dv), q.dtype)
    _, o = lax.scan(step, S0, xs)
    return jnp.moveaxis(o, 0, 1).swapaxes(2, 3).reshape(B, T, H, Dv)

def first_inputs(seed: int = 0) -> dict:
    key = jax.random.key(seed)
    ks = jax.random.split(key, 24)
    f32 = jnp.float32
    L = DEPTH

    def nrm(k, shape, scale):
        return jax.random.normal(k, shape, f32) * scale

    def gain(k, shape):
        return 1.0 + 0.05 * jax.random.normal(k, shape, f32)

    dt = jnp.exp(jax.random.uniform(ks[13], (L, DN_HEADS), f32, math.log(1e-3), math.log(1e-1)))
    return {
        "x": jax.random.normal(ks[0], (BATCH, SEQ, D_MODEL), f32),
        "ffn1_norm": gain(ks[1], (L, D_MODEL)),
        "ffn1_w_gate": nrm(ks[2], (L, D_MODEL, D_FF), D_MODEL ** -0.5),
        "ffn1_w_up": nrm(ks[3], (L, D_MODEL, D_FF), D_MODEL ** -0.5),
        "ffn1_w_down": nrm(ks[4], (L, D_FF, D_MODEL), D_FF ** -0.5),
        "mix_norm": gain(ks[5], (L, D_MODEL)),
        "w_in": nrm(ks[6], (L, D_MODEL, D_IN), D_MODEL ** -0.5),
        "gm_ln_g": gain(ks[7], (L, GM_WIDTH)),
        "gm_ln_b": nrm(ks[8], (L, GM_WIDTH), 0.02),
        "gm_w_s": nrm(ks[9], (L, GM_GROUPS, GM_BLOCK, GM_BLOCK), GM_BLOCK ** -0.5),
        "gm_b_s": 1.0 + nrm(ks[10], (L, GM_GROUPS, GM_BLOCK), 0.1),
        "dn_conv_w": nrm(ks[11], (L, DN_CONV, 3 * DN_WIDTH), DN_CONV ** -0.5),
        "dn_a_log": jnp.log(jax.random.uniform(ks[12], (L, DN_HEADS), f32, 1.0, 16.0)),
        "dn_dt_bias": dt + jnp.log(-jnp.expm1(-dt)),
        "dn_norm": gain(ks[14], (L, DN_HEAD_DIM)),
        "w_out": nrm(ks[15], (L, D_MIX, D_MODEL), D_MIX ** -0.5),
        "ffn2_norm": gain(ks[16], (L, D_MODEL)),
        "ffn2_w_gate": nrm(ks[17], (L, D_MODEL, D_FF), D_MODEL ** -0.5),
        "ffn2_w_up": nrm(ks[18], (L, D_MODEL, D_FF), D_MODEL ** -0.5),
        "ffn2_w_down": nrm(ks[19], (L, D_FF, D_MODEL), D_FF ** -0.5),
        "final_norm": gain(ks[20], (D_MODEL,)),
    }

def first_block(x, ffn1_norm, ffn1_w_gate, ffn1_w_up, ffn1_w_down, mix_norm, w_in,
              gm_ln_g, gm_ln_b, gm_w_s, gm_b_s, dn_conv_w, dn_a_log, dn_dt_bias, dn_norm,
              w_out, ffn2_norm, ffn2_w_gate, ffn2_w_up, ffn2_w_down, final_norm):
    B, T, _ = x.shape
    split_at = [GM_WIDTH, 2 * GM_WIDTH, 2 * GM_WIDTH + 3 * DN_WIDTH,
                2 * GM_WIDTH + 4 * DN_WIDTH, 2 * GM_WIDTH + 4 * DN_WIDTH + DN_HEADS]
    for l in range(DEPTH):
        x = x + 0.5 * swiglu(rmsnorm(x, ffn1_norm[l]), ffn1_w_gate[l], ffn1_w_up[l], ffn1_w_down[l])

        h = rmsnorm(x, mix_norm[l])
        p = h @ w_in[l]
        u_a, v_a, qkv, z, b_raw, a_raw = jnp.split(p, split_at, axis=-1)

        y_a = spatial_gating(jax.nn.gelu(u_a), jax.nn.gelu(v_a), gm_w_s[l], gm_b_s[l],
                             gm_ln_g[l], gm_ln_b[l])

        qkv = jax.nn.silu(causal_dwconv(qkv, dn_conv_w[l])).astype(jnp.float32)
        q, k, v = jnp.split(qkv, 3, axis=-1)
        q = l2norm(q.reshape(B, T, DN_HEADS, DN_HEAD_DIM))
        k = l2norm(k.reshape(B, T, DN_HEADS, DN_HEAD_DIM))
        v = v.reshape(B, T, DN_HEADS, DN_HEAD_DIM)
        beta = jax.nn.sigmoid(b_raw.astype(jnp.float32))
        g = -jnp.exp(dn_a_log[l].astype(jnp.float32)) * jax.nn.softplus(
            a_raw.astype(jnp.float32) + dn_dt_bias[l].astype(jnp.float32))
        o = gated_delta_rule(q, k, v, beta, g)
        zg = jax.nn.silu(z.astype(jnp.float32)).reshape(B, T, DN_HEADS, DN_HEAD_DIM)
        y_b = (rmsnorm(o, dn_norm[l]) * zg).reshape(B, T, DN_WIDTH).astype(x.dtype)

        x = x + jnp.concatenate([y_a, y_b], axis=-1) @ w_out[l]

        x = x + 0.5 * swiglu(rmsnorm(x, ffn2_norm[l]), ffn2_w_gate[l], ffn2_w_up[l], ffn2_w_down[l])
    return rmsnorm(x, final_norm)


MEM_LEN = 256
FFN_RES_WEIGHT = 0.5
CONV_A_WIDTH = D_MODEL
CONV_A_K = 3
SSM_D_INNER = 2 * D_MODEL
SSM_HEAD_DIM = 64
SSM_HEADS = SSM_D_INNER // SSM_HEAD_DIM
SSM_GROUPS = 4
SSM_STATE = 128
SSM_CONV_K = 4
SSM_CHUNK = 128
SSM_CONV_CH = SSM_D_INNER + 2 * SSM_GROUPS * SSM_STATE
XATTN_HEADS = 4
XATTN_HEAD_DIM = D_MODEL // XATTN_HEADS
XATTN_SCALE = 1.0 / math.sqrt(XATTN_HEAD_DIM)
IN_SIZES = (CONV_A_WIDTH, CONV_A_WIDTH, CONV_A_WIDTH,
            SSM_D_INNER, SSM_CONV_CH, SSM_HEADS,
            D_MODEL, D_MODEL)
D_IN_PROJ = sum(IN_SIZES)
IN_SPLITS = tuple(int(v) for v in np.cumsum(IN_SIZES)[:-1])


def rmsnorm_2(x, g):
    xf = x.astype(jnp.float32)
    y = xf * lax.rsqrt(jnp.mean(xf * xf, axis=-1, keepdims=True) + EPS)
    return (y * g.astype(jnp.float32)).astype(x.dtype)

def swiglu_2(u, w_gate_up, w_down):
    gate, up = jnp.split(u @ w_gate_up, 2, axis=-1)
    return (jax.nn.silu(gate) * up) @ w_down

def causal_dwconv_2(x, w):
    k, c = w.shape
    return lax.conv_general_dilated(
        x, w[:, None, :].astype(x.dtype), window_strides=(1,),
        padding=[(k - 1, 0)], dimension_numbers=('NWC', 'WIO', 'NWC'),
        feature_group_count=c)

def short_conv_branch(b_gate, c_gate, v, conv_w, w_out):
    return (b_gate * causal_dwconv_2(c_gate * v, conv_w)) @ w_out

def ssd_chunked(xh, dt, a, bm, cm):
    b, s, h, p = xh.shape
    g, n = bm.shape[-2:]
    k = h // g
    l = SSM_CHUNK
    c = s // l
    x = (xh.astype(jnp.float32) * dt[..., None]).reshape(b, c, l, g, k, p)
    la = (dt * a).reshape(b, c, l, g, k).transpose(0, 1, 3, 4, 2)
    acs = jnp.cumsum(la, axis=-1)
    bc = bm.astype(jnp.float32).reshape(b, c, l, g, n)
    cc = cm.astype(jnp.float32).reshape(b, c, l, g, n)
    seg = acs[..., :, None] - acs[..., None, :]
    causal = jnp.tril(jnp.ones((l, l), dtype=bool))
    decay = jnp.exp(jnp.where(causal, seg, -jnp.inf))
    cb = jnp.einsum('bclgn,bcsgn->bcgls', cc, bc)
    y_diag = jnp.einsum('bcgls,bcgkls,bcsgkp->bclgkp', cb, decay, x)
    decay_to_end = jnp.exp(acs[..., -1:] - acs)
    states = jnp.einsum('bclgn,bcgkl,bclgkp->bcgkpn', bc, decay_to_end, x)
    chunk_decay = jnp.exp(acs[..., -1])

    def step(carry, inp):
        st, dec = inp
        return carry * dec[..., None, None] + st, carry

    init = jnp.zeros((b, g, k, p, n), jnp.float32)
    _, prev = lax.scan(step, init, (jnp.moveaxis(states, 1, 0), jnp.moveaxis(chunk_decay, 1, 0)))
    prev = jnp.moveaxis(prev, 0, 1)
    y_off = jnp.einsum('bclgn,bcgkpn,bcgkl->bclgkp', cc, prev, jnp.exp(acs))
    return (y_diag + y_off).reshape(b, s, h, p)

def mamba2_branch(z, xbc, dt_raw, conv_w, conv_b, dt_bias, a_log, d_skip, norm_g, w_out):
    xbc = jax.nn.silu(causal_dwconv_2(xbc, conv_w) + conv_b.astype(xbc.dtype))
    xs, bm, cm = jnp.split(xbc, (SSM_D_INNER, SSM_D_INNER + SSM_GROUPS * SSM_STATE), axis=-1)
    b, s, _ = xs.shape
    xh = xs.reshape(b, s, SSM_HEADS, SSM_HEAD_DIM)
    dt = jax.nn.softplus(dt_raw.astype(jnp.float32) + dt_bias.astype(jnp.float32))
    a = -jnp.exp(a_log.astype(jnp.float32))
    y = ssd_chunked(xh, dt, a,
                    bm.reshape(b, s, SSM_GROUPS, SSM_STATE),
                    cm.reshape(b, s, SSM_GROUPS, SSM_STATE))
    y = y + d_skip.astype(jnp.float32)[:, None] * xh.astype(jnp.float32)
    yg = (y.reshape(b, s, SSM_D_INNER) * jax.nn.silu(z.astype(jnp.float32)))
    yg = yg.reshape(b, s, SSM_GROUPS, SSM_D_INNER // SSM_GROUPS)
    yg = yg * lax.rsqrt(jnp.mean(yg * yg, axis=-1, keepdims=True) + EPS)
    y = (yg.reshape(b, s, SSM_D_INNER) * norm_g.astype(jnp.float32)).astype(z.dtype)
    return y @ w_out

def memory_cross_attention(u, mem_n, w_q, w_kv, w_o):
    b, s, _ = u.shape
    m = mem_n.shape[1]
    q = (u @ w_q).reshape(b, s, XATTN_HEADS, XATTN_HEAD_DIM)
    k, v = jnp.split(mem_n @ w_kv, 2, axis=-1)
    k = k.reshape(b, m, XATTN_HEADS, XATTN_HEAD_DIM)
    v = v.reshape(b, m, XATTN_HEADS, XATTN_HEAD_DIM)
    scores = jnp.einsum('bshd,bmhd->bhsm', q, k).astype(jnp.float32) * XATTN_SCALE
    probs = jax.nn.softmax(scores, axis=-1).astype(v.dtype)
    o = jnp.einsum('bhsm,bmhd->bshd', probs, v).reshape(b, s, D_MODEL)
    return o @ w_o

def second_inputs(seed: int = 0) -> dict:
    key = jax.random.key(seed)
    ks = iter(jax.random.split(key, 40))

    def w(shape, fan_in):
        return jax.random.normal(next(ks), shape, jnp.float32) * (fan_in ** -0.5)

    def gain(shape):
        return 1.0 + 0.02 * jax.random.normal(next(ks), shape, jnp.float32)

    L = DEPTH
    x = jax.random.normal(next(ks), (BATCH, SEQ, D_MODEL), jnp.float32)
    mem = jax.random.normal(next(ks), (BATCH, MEM_LEN, D_MODEL), jnp.float32)
    dt0 = jnp.exp(jax.random.uniform(next(ks), (L, SSM_HEADS), jnp.float32,
                                     math.log(1e-3), math.log(1e-1)))
    dt_bias = dt0 + jnp.log(-jnp.expm1(-dt0))
    a_log = jnp.log(jax.random.uniform(next(ks), (L, SSM_HEADS), jnp.float32, 1.0, 16.0))
    return {
        "x": x,
        "mem": mem,
        "ffn1_norm": gain((L, D_MODEL)),
        "ffn1_w_gate_up": w((L, D_MODEL, 2 * D_FF), D_MODEL),
        "ffn1_w_down": w((L, D_FF, D_MODEL), D_FF),
        "mix_norm": gain((L, D_MODEL)),
        "w_in": w((L, D_MODEL, D_IN_PROJ), D_MODEL),
        "conv_a_w": w((L, CONV_A_K, CONV_A_WIDTH), CONV_A_K),
        "w_out_a": w((L, CONV_A_WIDTH, D_MODEL), CONV_A_WIDTH),
        "ssm_conv_w": w((L, SSM_CONV_K, SSM_CONV_CH), SSM_CONV_K),
        "ssm_conv_b": 0.02 * jax.random.normal(next(ks), (L, SSM_CONV_CH), jnp.float32),
        "ssm_dt_bias": dt_bias,
        "ssm_a_log": a_log,
        "ssm_d": gain((L, SSM_HEADS)),
        "ssm_norm": gain((L, SSM_D_INNER)),
        "w_out_ssm": w((L, SSM_D_INNER, D_MODEL), SSM_D_INNER),
        "w_mix_out": w((L, D_MODEL, D_MODEL), D_MODEL),
        "xattn_norm": gain((L, D_MODEL)),
        "mem_norm": gain((L, D_MODEL)),
        "w_q": w((L, D_MODEL, D_MODEL), D_MODEL),
        "w_kv": w((L, D_MODEL, 2 * D_MODEL), D_MODEL),
        "w_o_x": w((L, D_MODEL, D_MODEL), D_MODEL),
        "ffn2_norm": gain((L, D_MODEL)),
        "ffn2_w_gate_up": w((L, D_MODEL, 2 * D_FF), D_MODEL),
        "ffn2_w_down": w((L, D_FF, D_MODEL), D_FF),
        "final_norm": gain((D_MODEL,)),
    }

def second_block(x, mem, ffn1_norm, ffn1_w_gate_up, ffn1_w_down, mix_norm, w_in, conv_a_w,
              w_out_a, ssm_conv_w, ssm_conv_b, ssm_dt_bias, ssm_a_log, ssm_d, ssm_norm,
              w_out_ssm, w_mix_out, xattn_norm, mem_norm, w_q, w_kv, w_o_x,
              ffn2_norm, ffn2_w_gate_up, ffn2_w_down, final_norm):
    h = x
    for i in range(DEPTH):
        h = h + FFN_RES_WEIGHT * swiglu_2(rmsnorm_2(h, ffn1_norm[i]), ffn1_w_gate_up[i], ffn1_w_down[i])
        u = rmsnorm_2(h, mix_norm[i])
        proj = u @ w_in[i]
        a_b, a_c, a_v, z, xbc, dt_raw, g_a, g_b = jnp.split(proj, IN_SPLITS, axis=-1)
        y_a = short_conv_branch(a_b, a_c, a_v, conv_a_w[i], w_out_a[i])
        y_b = mamba2_branch(z, xbc, dt_raw, ssm_conv_w[i], ssm_conv_b[i], ssm_dt_bias[i],
                            ssm_a_log[i], ssm_d[i], ssm_norm[i], w_out_ssm[i])
        merged = jax.nn.sigmoid(g_a) * y_a + jax.nn.sigmoid(g_b) * y_b
        h = h + merged @ w_mix_out[i]
        h = h + memory_cross_attention(rmsnorm_2(h, xattn_norm[i]), rmsnorm_2(mem, mem_norm[i]),
                                       w_q[i], w_kv[i], w_o_x[i])
        h = h + FFN_RES_WEIGHT * swiglu_2(rmsnorm_2(h, ffn2_norm[i]), ffn2_w_gate_up[i], ffn2_w_down[i])
    return rmsnorm_2(h, final_norm)


def setup_inputs(seed=0):
    out = dict(first_inputs(seed))
    for name, value in second_inputs(seed + 1).items():
        if name != "x":
            out[name + "_2"] = value
    return out


def reference(
    x, ffn1_norm, ffn1_w_gate, ffn1_w_up, ffn1_w_down, mix_norm, w_in, gm_ln_g, gm_ln_b, gm_w_s,
    gm_b_s, dn_conv_w, dn_a_log, dn_dt_bias, dn_norm, w_out, ffn2_norm, ffn2_w_gate, ffn2_w_up,
    ffn2_w_down, final_norm, mem_2, ffn1_norm_2, ffn1_w_gate_up_2, ffn1_w_down_2, mix_norm_2,
    w_in_2, conv_a_w_2, w_out_a_2, ssm_conv_w_2, ssm_conv_b_2, ssm_dt_bias_2, ssm_a_log_2,
    ssm_d_2, ssm_norm_2, w_out_ssm_2, w_mix_out_2, xattn_norm_2, mem_norm_2, w_q_2, w_kv_2,
    w_o_x_2, ffn2_norm_2, ffn2_w_gate_up_2, ffn2_w_down_2, final_norm_2,
):
    x = first_block(
        x, ffn1_norm, ffn1_w_gate, ffn1_w_up, ffn1_w_down, mix_norm, w_in, gm_ln_g, gm_ln_b,
        gm_w_s, gm_b_s, dn_conv_w, dn_a_log, dn_dt_bias, dn_norm, w_out, ffn2_norm, ffn2_w_gate,
        ffn2_w_up, ffn2_w_down, final_norm,
    )
    return second_block(
        x, mem_2, ffn1_norm_2, ffn1_w_gate_up_2, ffn1_w_down_2, mix_norm_2, w_in_2, conv_a_w_2,
        w_out_a_2, ssm_conv_w_2, ssm_conv_b_2, ssm_dt_bias_2, ssm_a_log_2, ssm_d_2, ssm_norm_2,
        w_out_ssm_2, w_mix_out_2, xattn_norm_2, mem_norm_2, w_q_2, w_kv_2, w_o_x_2, ffn2_norm_2,
        ffn2_w_gate_up_2, ffn2_w_down_2, final_norm_2,
    )


_drawn_inputs = setup_inputs


def setup_inputs(seed=0):
    import zlib

    import numpy as np

    out = dict(_drawn_inputs(seed))
    spreads = {}
    factors = {'gm_ln_g': 2.677,
     'gm_ln_b': 6.944,
     'ffn1_norm_2': 5.396,
     'mix_norm_2': 2.768,
     'ssm_conv_b_2': 4.702,
     'ssm_d_2': 64.0,
     'ssm_norm_2': 19.15,
     'xattn_norm_2': 8.0,
     'mem_norm_2': 8.0,
     'ffn2_norm_2': 21.521,
     'final_norm_2': 7.933}
    for name, (base, spread) in spreads.items():
        noise = np.random.default_rng([zlib.crc32(name.encode()), seed]).standard_normal(out[name].shape)
        drawn = base * np.exp(spread * noise) if base else spread * noise
        out[name] = __import__('jax').numpy.asarray(drawn.astype(out[name].dtype))
    for name, factor in factors.items():
        out[name] = (out[name] * factor).astype(out[name].dtype)
    return out
```

```python
from contextlib import ExitStack

import numpy as np
import concourse.bass as bass
from concourse import mybir

F32 = mybir.dt.float32
F32R = mybir.dt.float32r
BF16 = mybir.dt.bfloat16
ALU = mybir.AluOpType
ACT = mybir.ActivationFunctionType

P = 128
T = 256
NT = T // P
D = 1024
KD = D // P
DFF = 2816
KFF = DFF // P
CH = 256
NCH = DFF // CH
RING = 4
SLOT = 2048
EPS = 1e-6

GM_G, GM_C, GM_W = 8, 64, 512
H1, DH1 = 4, 128
TAPS1 = 4
CONV_A_K = 3
SSM_IN, SSM_HD, SSM_H, SSM_G, SSM_N = 2048, 64, 32, 4, 128
HPG = SSM_H // SSM_G
SSM_CONV_K = 4
XH, XDH, MEM = 4, 256, 256

SOLVE_LEVELS = [2 ** i for i in range(7)]


class Unit:

    def __init__(self, name, granules, g):
        self.name, self.granules, self.g, self.n = name, granules, g, 512


def plan_stream():
    units, count = {}, [0]
    full = [(0, 1, 2, 3), (4, 5, 6, 7)]

    def add(name, granules=full):
        units[name] = Unit(name, granules, count[0])
        count[0] += len(granules)

    def add_ffn(f):
        for c in range(NCH):
            add(f"ffn{f}.up{c}")
        for half in range(2):
            add(f"ffn{f}.down{half}.0")
            add(f"ffn{f}.down{half}.1", [(8, 9, 10, 11), (12, 13, 14, 15)])
            add(f"ffn{f}.down{half}.2", [(16, 17, 18, 19), (20, 21)])

    add_ffn(0)
    for name in ("k", "q", "v", "gv", "gu", "z"):
        add("m1." + name)
    add("m1.out_a", [(0, 1, 2, 3), (0, 1, 2, 3)])
    add("m1.out_b", [(4, 5, 6, 7), (4, 5, 6, 7)])
    add_ffn(1)
    add_ffn(2)
    for name in ("B", "C", "x0", "x1", "x2", "x3", "c0", "v0", "b0", "c1", "v1", "b1",
                 "z0", "z1", "z2", "z3", "ga0", "ga1", "gb0", "gb1", "oa0", "oa1"):
        add("m2." + name)
    for half in range(2):
        add(f"m2.os{half}.0")
        add(f"m2.os{half}.1", [(8, 9, 10, 11), (12, 13, 14, 15)])
    first, second = [(0, 1, 2, 3)] * 2, [(4, 5, 6, 7)] * 2
    add("m2.mix_a", first)
    add("m2.mix_b", second)
    for name in ("k0", "k1", "q0", "q1", "v0", "v1"):
        add("xa." + name)
    add("xa.o_a", first)
    add("xa.o_b", second)
    add_ffn(3)
    return units


B_FFN0, B_MIX1, B_FFN1, B_FFN2, B_MIX2, B_XA, B_FFN3, B_OUT = range(8)
FFN_NORM = (B_FFN0, B_FFN1, B_FFN2, B_FFN3)


class Signals:

    def __init__(self, nc, ctx):
        self.nc, self.ctx, self.made = nc, ctx, {}

    def __getitem__(self, name):
        if name not in self.made:
            self.made[name] = self.ctx.enter_context(self.nc.semaphore(name))
        return self.made[name]


def build(nc, w, out, row_scratch):
    units = plan_stream()
    ctx = ExitStack()

    place = [nc.sbuf_base + 31 & ~31]

    def sb(name, shape, dt=F32):
        size = int(np.prod(shape[1:])) * {BF16: 2, mybir.dt.uint8: 1}.get(dt, 4)
        at = place[0]
        place[0] += size + 31 & ~31
        return nc.alloc_sbuf_tensor_at(name, shape, dt, offset=at)

    ident = sb("ident", [P, P])
    up_to = sb("up_to", [P, P])
    ones = sb("ones", [P, P])
    gain = sb("gain", [P, 7, KD])
    dn_gain = sb("dn_gain", [P, 1])
    ss = sb("ss", [P, NT, 2])
    ssg = sb("ssg", [P, NT, 2])
    ms = sb("ms", [P, NT])
    msg = sb("msg", [P, NT])
    rstd = sb("rstd", [P, NT])
    rstd_final = sb("rstd_final", [P, NT])
    rstd_both = sb("rstd_both", [P, NT])
    minus_half = sb("minus_half", [P, NT * H1])
    junk = sb("junk", [P, 512], BF16)

    gm_r = sb("gm_r", [P, NT])
    sb_small = {
        "m1_conv": sb("m1_conv", [P, 12, TAPS1]),
        "gm_bias": sb("gm_bias", [P, GM_G]),
        "dn_rows": sb("dn_rows", [P, 2, H1]),
        "ba_raw": sb("ba_raw", [P, KD, 8]),
        "ba_hi": sb("ba_hi", [P, KD, 8], F32R),
        "ba_lo": sb("ba_lo", [P, KD, 8], F32R),
        "ba": sb("ba", [P, NT, 8]),
        "stats": sb("stats", [P, NT, 6]),
        "mv": sb("mv", [P, NT, 2]),
    }
    m2_small = {
        "ssm_conv": sb("ssm_conv_w", [P, 24, SSM_CONV_K]),
        "ssm_bias": sb("ssm_bias", [P, 24]),
        "conv_a": sb("conv_a_w", [P, KD, CONV_A_K]),
        "ssm_gain": sb("ssm_gain", [P, SSM_IN // P]),
        "ssm_rows": sb("ssm_rows", [P, 3, SSM_H]),
    }
    mem_gain = sb("mem_gain", [P, KD])
    mem_ss = sb("mem_ss", [P, 2 * NT])[:, :]
    mem_r = sb("mem_r", [P, NT])[:, :]

    raw = sb("raw", [P, RING, SLOT])
    whi = sb("whi", [P, RING, SLOT], F32R)
    wlo = sb("wlo", [P, RING, SLOT], F32R)
    x = sb("x", [P, NT, D])
    xT_hi = sb("xT_hi", [P, KD, T], F32R)
    xT_lo = sb("xT_lo", [P, KD, T], F32R)
    scratch = place[0]
    CELL = 4096

    def cell(name, n, shape, dt=F32, plus=0):
        return nc.alloc_sbuf_tensor_at(name, shape, dt, offset=scratch + n * CELL + plus)

    hid_hi = cell("hid_hi", 0, [P, KFF, T], F32R)
    hid_lo = cell("hid_lo", 6, [P, KFF, T], F32R)
    gate_act = cell("gate_act", 12, [P, NT, CH])
    hidden = cell("hidden", 13, [P, 2, NT, CH])
    gfinal_row = cell("gfinal_row", 23, [P, D])
    gfinal2_row = cell("gfinal2_row", 23, [P, D])
    assert scratch + 24 * CELL <= 229344, scratch

    acc = nc.alloc_psum_tensor("acc", [P, 4, 512], F32)
    work = nc.alloc_psum_tensor("work", [P, 4, 512], F32)

    def sem(name):
        return ctx.enter_context(nc.semaphore(name))

    x_loaded, consts_loaded, params_loaded = sem("x_loaded"), sem("consts_loaded"), sem("params_loaded")
    raw_ready = [sem(f"raw_ready{s}") for s in range(RING)]
    hi_ready = sem("hi_ready")
    lo_even, lo_odd = sem("lo_even"), sem("lo_odd")
    gran_done = sem("gran_done")
    resid_done = sem("resid_done")
    xt_done = sem("xt_done")
    xhi_done, xlo_done = sem("xhi_done"), sem("xlo_done")
    sq_done, squares = sem("sq_done"), sem("squares")
    pool_chain = sem("pool_chain")
    rstd_ready = sem("rstd_ready")
    half_const = sem("half_const")
    silu_done, h_done = sem("silu_done"), sem("h_done")
    hidt_done, hidhi_done, hidlo_done = sem("hidt_done"), sem("hidhi_done"), sem("hidlo_done")
    final1_loaded = sem("final1_loaded")
    final_gained, gained_squared, x_rescaled = sem("final_gained"), sem("gained_squared"), sem("x_rescaled")
    fin_done, out_stored = sem("fin_done"), sem("out_stored")

    block = ctx.enter_context(nc.Block())

    def wait(eng, s, value, it=None, per=0):
        eng.wait_ge(s, value if it is None else it * per + value)

    def wait_lo(eng, g, it=None):
        wait(eng, lo_odd if g % 2 else lo_even, g // 2 + 1, it, RING // 2)

    def wait_unit_done(eng, u, it=None):
        wait(eng, gran_done, u.g + len(u.granules), it, RING)

    def granule(buf, u, i):
        kts = u.granules[i]
        return buf[:, (u.g + i) % RING, 0:len(kts) * u.n].rearrange("p (k n) -> p k n", n=u.n)

    def pair(q):
        return [acc[:, 2 * q + t, :] for t in range(NT)]

    def load(sp, u, i, tile, it=None):
        g = u.g + i
        if g >= RING:
            wait_lo(sp, g - RING, it)
        kt0, n = u.granules[i][0] * u.n, len(u.granules[i]) * u.n
        sp.dma_start(raw[:, g % RING, 0:n], tile[:, kt0:kt0 + n]).then_inc(raw_ready[g % RING], 16)

    def split_hi(act, u, i, it=None):
        g = u.g + i
        wait(act, raw_ready[g % RING], 16 * (g // RING + 1), it, 16)
        if g >= RING:
            wait(act, gran_done, g - RING + 1, it, RING)
        act.activation(granule(whi, u, i), granule(raw, u, i), ACT.Copy).then_inc(hi_ready, 1)

    def split_lo(eng, u, i, it=None):
        g = u.g + i
        wait(eng, hi_ready, g + 1, it, RING)
        eng.tensor_tensor(granule(wlo, u, i), granule(raw, u, i), granule(whi, u, i).bitcast(F32),
                          ALU.subtract).then_inc(lo_odd if g % 2 else lo_even, 1)

    def multiply(pe, u, i, xhi, xlo, banks, start, stop, it=None, after_k=None, k0=0):
        wait_lo(pe, u.g + i, it)
        hi, lo = granule(whi, u, i), granule(wlo, u, i)
        kts = u.granules[i]
        for j, kt in enumerate(kts):
            kt -= k0
            for t in range(NT):
                tok = slice(t * P, (t + 1) * P)
                first, last = start and j == 0, stop and j == len(kts) - 1
                pe.matmul(banks[t][:, 0:u.n], xhi[:, kt, tok], hi[:, j, :], start=first, stop=False)
                pe.matmul(banks[t][:, 0:u.n], xhi[:, kt, tok], lo[:, j, :], start=False, stop=False)
                mm = pe.matmul(banks[t][:, 0:u.n], xlo[:, kt, tok], hi[:, j, :], start=False, stop=last)
            if after_k is not None and j in after_k:
                after_k[j]()
        mm.then_inc(gran_done, 1)

    def transpose_x(pe, b, half):
        if b == 0:
            if half == 0:
                pe.wait_ge(x_loaded, 16)
                pe.wait_ge(consts_loaded, 16 * N_CONSTS)
        elif b == B_FFN2:
            pe.wait_ge(final_gained, half + 1)
        else:
            pe.wait_ge(resid_done, 2 * (b - 1) + half + 1)
        for k in range(4):
            for t in range(NT):
                bank = work[:, 2 * half + k // 2, :]
                at = (k % 2) * T + t * P
                c = half * 512 + k * P
                tr = pe.transpose(bank[:, at:at + P], x[:, t, c:c + P], ident[:, :])
        tr.then_inc(xt_done, 1)

    def xt_tile(half, k):
        return work[:, 2 * half + k // 2, (k % 2) * T:(k % 2 + 1) * T]

    squared = [0]

    def square(act, src, total):
        if squared[0]:
            act.wait_ge(squares, squared[0])
        act.activation(junk[:, 0:src.shape[-1]], src, ACT.Square, accum_out=total).then_inc(squares, 1)
        squared[0] += 1

    def square_x(act, b, half):
        if b:
            act.wait_ge(resid_done, 2 * (b - 1) + half + 1)
            act.wait_ge(rstd_ready, b)
        else:
            act.wait_ge(x_loaded, 16)
        for t in range(NT):
            square(act, x[:, t, half * 512:(half + 1) * 512], ss[:, t, half:half + 1])
        act.wait_ge(squares, squared[0])
        act.sem_inc(sq_done, 1)

    def round_xt(act, b, half):
        act.wait_ge(xt_done, 2 * b + half + 1)
        for k in range(4):
            kt = 4 * half + k
            act.activation(xT_hi[:, kt, :], xt_tile(half, k), ACT.Copy,
                           scale=gain[:, b, kt:kt + 1]).then_inc(xhi_done, 1)

    def rest_xt(dve, b, half):
        for k in range(4):
            kt = 4 * half + k
            if k % 2 == 0:
                dve.wait_ge(xhi_done, 8 * b + kt + 2)
            st = dve.scalar_tensor_tensor(out=xT_lo[:, kt, :], in0=xt_tile(half, k),
                                          scalar=gain[:, b, kt:kt + 1],
                                          in1=xT_hi[:, kt, :].bitcast(F32), op0=ALU.mult, op1=ALU.subtract)
        st.then_inc(xlo_done, 1)

    def residual(dve, b, half, u, banks, alpha):
        residual_half(dve, b, half, u.g + len(u.granules), banks, alpha)

    def residual_half(dve, b, half, granules, banks, alpha):
        dve.wait_ge(gran_done, granules)
        if b == B_MIX2:
            dve.wait_ge(x_rescaled, NT)
        dve.wait_ge(sq_done, 2 * b)
        for t in range(NT):
            c = slice(half * 512, (half + 1) * 512)
            st = dve.scalar_tensor_tensor(out=x[:, t, c], in0=banks[t], scalar=alpha, in1=x[:, t, c],
                                          op0=ALU.mult, op1=ALU.add)
        st.then_inc(resid_done, 1)

    def apply_final1(dve, half):
        c = slice(half * 512, (half + 1) * 512)
        dve.wait_ge(final1_loaded, 16)
        dve.wait_ge(sq_done, 2 * B_FFN2 + half + 1)
        for t in range(NT):
            tt = dve.tensor_tensor(x[:, t, c], x[:, t, c], gfinal_row[:, c], ALU.mult)
        tt.then_inc(final_gained, 1)

    def square_gained(act, half):
        act.wait_ge(final_gained, half + 1)
        for t in range(NT):
            square(act, x[:, t, half * 512:(half + 1) * 512], ssg[:, t, half:half + 1])
        act.wait_ge(squares, squared[0])
        act.sem_inc(gained_squared, 1)

    def rescale_x(act):
        act.wait_ge(xt_done, 2 * B_FFN2 + 2)
        for t in range(NT):
            act.activation(x[:, t, :], x[:, t, :], ACT.Copy, scale=rstd_final[:, t:t + 1]).then_inc(x_rescaled, 1)

    chained = [0]

    def link(pool, op):
        op.then_inc(pool_chain, 1)
        chained[0] += 1
        pool.wait_ge(pool_chain, chained[0])

    def reciprocal_rms(pool, b):
        pool.wait_ge(sq_done, 2 * b + 2)
        link(pool, pool.tensor_tensor(ms[:, :], ss[:, :, 0], ss[:, :, 1], ALU.add))
        link(pool, pool.tensor_scalar(ms[:, :], ms[:, :], 1.0 / D, EPS, ALU.mult, ALU.add))
        if b != B_FFN2:
            pool.tensor_tensor(rstd[:, :], ms[:, :], minus_half[:, 0:NT], ALU.pow).then_inc(rstd_ready, 1)
            return
        link(pool, pool.tensor_tensor(rstd_final[:, :], ms[:, :], minus_half[:, 0:NT], ALU.pow))
        pool.wait_ge(gained_squared, 2)
        link(pool, pool.tensor_tensor(msg[:, :], ssg[:, :, 0], ssg[:, :, 1], ALU.add))
        link(pool, pool.tensor_tensor(msg[:, :], msg[:, :], rstd_final[:, :], ALU.mult))
        link(pool, pool.tensor_tensor(msg[:, :], msg[:, :], rstd_final[:, :], ALU.mult))
        link(pool, pool.tensor_scalar(msg[:, :], msg[:, :], 1.0 / D, EPS, ALU.mult, ALU.add))
        link(pool, pool.tensor_tensor(rstd_both[:, :], msg[:, :], minus_half[:, 0:NT], ALU.pow))
        pool.tensor_tensor(rstd[:, :], rstd_both[:, :], rstd_final[:, :], ALU.mult).then_inc(rstd_ready, 1)

    TURNS = 3

    def ffn_loads(sp, f):
        up_tiles, down_tiles = w[f"t_ffn{f}_up"], w[f"t_ffn{f}_down"]

        def up(c, it=None):
            tile = up_tiles[c] if it is None else up_tiles[bass.ds(it * 2 + c, 1)].rearrange("a p n -> (a p) n")
            for i in range(2):
                load(sp, units[f"ffn{f}.up{c}"], i, tile, it)

        up(0)
        up(1)
        with sp.Fori(0, 4) as it:
            up(2, it)
            up(3, it)
        up(10)
        for half in range(2):
            for j in range(3):
                for i in range(2):
                    load(sp, units[f"ffn{f}.down{half}.{j}"], i, down_tiles[half])

    ffn_off = (0, 1, 0, 1)

    def ffn_banks(f, c):
        return pair((c + ffn_off[f]) % 2)

    def ffn_hidden_t(pe, f, c, it=None):
        n = NCH * f + c
        wait(pe, h_done, 2 * (n + 1), it, 4)
        if n >= 2:
            wait(pe, hidlo_done, n - 1, it, 2)
        bank = work[:, c % 2, :]
        for kt in range(2):
            for t in range(NT):
                tr = pe.transpose(bank[:, kt * T + t * P:kt * T + (t + 1) * P],
                                  hidden[:, c % 2, t, kt * P:(kt + 1) * P], ident[:, :])
        tr.then_inc(hidt_done, 1)

    def ffn_tensor(pe, f):
        b = FFN_NORM[f]

        def up(c, it=None, halfway=None, after_k=None):
            n = NCH * f + c
            u = units[f"ffn{f}.up{c}"]
            if c >= 2:
                wait(pe, h_done, 2 * (n - 1), it, 4)
            multiply(pe, u, 0, xT_hi, xT_lo, ffn_banks(f, c), True, False, it, after_k)
            if halfway is not None:
                halfway()
            multiply(pe, u, 1, xT_hi, xT_lo, ffn_banks(f, c), False, True, it)

        pe.wait_ge(xlo_done, 2 * b + 1)

        def second_half():
            transpose_x(pe, b, 1)

        up(0, after_k={1: second_half}, halfway=lambda: pe.wait_ge(xlo_done, 2 * b + 2))
        up(1, halfway=lambda: ffn_hidden_t(pe, f, 0))
        up(2, halfway=lambda: ffn_hidden_t(pe, f, 1))
        with pe.Fori(0, TURNS) as it:
            up(3, it, halfway=lambda: ffn_hidden_t(pe, f, 2, it))
            up(4, it, halfway=lambda: ffn_hidden_t(pe, f, 3, it))
        up(9, halfway=lambda: ffn_hidden_t(pe, f, 8))
        up(10, halfway=lambda: ffn_hidden_t(pe, f, 9))
        for half in range(2):
            banks = ffn_banks(f, NCH + half)
            if half == 0:
                pe.wait_ge(h_done, 2 * (NCH * f + 10))
            else:
                pe.wait_ge(h_done, 2 * (NCH * f + 11))
            for j in range(3):
                u = units[f"ffn{f}.down{half}.{j}"]
                if j == 2:
                    pe.wait_ge(hidlo_done, NCH * f + 11)
                elif half == 0 and j == 0:
                    pe.wait_ge(hidlo_done, NCH * f + 10)
                multiply(pe, u, 0, hid_hi, hid_lo, banks, j == 0, False)
                if half == 0 and j == 0:
                    ffn_hidden_t(pe, f, 10)
                if half == 1 and j == 0 and b + 1 != B_OUT:
                    transpose_x(pe, b + 1, 0)
                multiply(pe, u, 1, hid_hi, hid_lo, banks, False, j == 2)

    def ffn_scalar(act, f, next_units):
        b = FFN_NORM[f]

        def silu(c, it=None):
            n = NCH * f + c
            wait_unit_done(act, units[f"ffn{f}.up{c}"], it)
            if n:
                wait(act, h_done, 2 * n, it, 4)
            for t in range(NT):
                act.activation(gate_act[:, t, :], ffn_banks(f, c)[t][:, 0:CH], ACT.Silu,
                               scale=rstd[:, t:t + 1]).then_inc(silu_done, 1)

        def round_hidden(c, it=None):
            n = NCH * f + c
            wait(act, hidt_done, n + 1, it, 2)
            at = slice(2 * c, 2 * c + 2) if it is None else bass.ds(it * 4 + 2 * c, 2)
            act.activation(hid_hi[:, at, :].rearrange("p k t -> p (k t)"), work[:, c % 2, :],
                           ACT.Copy).then_inc(hidhi_done, 1)

        def step(c, it=None):
            silu(c - 1, it)
            split_hi(act, units[f"ffn{f}.up{c + 1}"], 0, it)
            round_hidden(c - 1, it)
            split_hi(act, units[f"ffn{f}.up{c + 1}"], 1, it)

        round_xt(act, b, 1)
        split_hi(act, units[f"ffn{f}.up1"], 0)
        split_hi(act, units[f"ffn{f}.up1"], 1)
        act.wait_ge(rstd_ready, b + 1)
        if b == B_FFN2:
            rescale_x(act)
        step(1)
        step(2)
        with act.Fori(0, TURNS) as it:
            step(3, it)
            step(4, it)
        step(9)
        down = [units[f"ffn{f}.down{half}.{j}"] for half in range(2) for j in range(3)] + next_units
        silu(9)
        split_hi(act, down[0], 0)
        round_hidden(9)
        split_hi(act, down[0], 1)
        silu(10)
        split_hi(act, down[1], 0)
        round_hidden(10)
        split_hi(act, down[1], 1)
        for j in (2, 3):
            split_hi(act, down[j], 0)
            split_hi(act, down[j], 1)
        square_x(act, b + 1, 0)
        if b + 1 == B_FFN2:
            square_gained(act, 0)
        split_hi(act, down[4], 0)
        if b + 1 != B_OUT:
            round_xt(act, b + 1, 0)
        split_hi(act, down[4], 1)
        for u in down[5:]:
            split_hi(act, u, 0)
            split_hi(act, u, 1)
        square_x(act, b + 1, 1)
        if b + 1 == B_FFN2:
            square_gained(act, 1)

    def ffn_vector(dve, f, next_units):
        b = FFN_NORM[f]

        def product(c, it=None):
            n = NCH * f + c
            if n >= 2:
                wait(dve, hidt_done, n - 1, it, 2)
            for t in range(NT):
                wait(dve, silu_done, 2 * n + t + 1, it, 4)
                dve.scalar_tensor_tensor(out=hidden[:, c % 2, t, :], in0=ffn_banks(f, c)[t][:, CH:2 * CH],
                                         scalar=rstd[:, t:t + 1], in1=gate_act[:, t, :],
                                         op0=ALU.mult, op1=ALU.mult).then_inc(h_done, 1)

        def rest_hidden(c, it=None):
            n = NCH * f + c
            wait(dve, hidhi_done, n + 1, it, 2)
            at = slice(2 * c, 2 * c + 2) if it is None else bass.ds(it * 4 + 2 * c, 2)
            flat = "p k t -> p (k t)"
            dve.tensor_tensor(hid_lo[:, at, :].rearrange(flat), work[:, c % 2, :],
                              hid_hi[:, at, :].rearrange(flat).bitcast(F32), ALU.subtract).then_inc(hidlo_done, 1)

        def step(c, it=None):
            product(c - 1, it)
            split_lo(dve, units[f"ffn{f}.up{c + 1}"], 0, it)
            rest_hidden(c - 1, it)

        rest_xt(dve, b, 1)
        split_lo(dve, units[f"ffn{f}.up1"], 0)
        step(1)
        step(2)
        with dve.Fori(0, TURNS) as it:
            step(3, it)
            step(4, it)
        step(9)
        down = [units[f"ffn{f}.down{half}.{j}"] for half in range(2) for j in range(3)] + next_units
        product(9)
        split_lo(dve, down[0], 0)
        rest_hidden(9)
        product(10)
        split_lo(dve, down[1], 0)
        rest_hidden(10)
        split_lo(dve, down[2], 0)
        split_lo(dve, down[3], 0)
        residual(dve, b + 1, 0, down[2], ffn_banks(f, NCH), 0.5)
        if b + 1 == B_FFN2:
            apply_final1(dve, 0)
        split_lo(dve, down[4], 0)
        if b + 1 != B_OUT:
            rest_xt(dve, b + 1, 0)
        for u in down[5:]:
            split_lo(dve, u, 0)
        residual(dve, b + 1, 1, down[5], ffn_banks(f, NCH + 1), 0.5)
        if b + 1 == B_FFN2:
            apply_final1(dve, 1)

    def ffn_pool(pool, f, next_units):
        def step(c, it=None):
            split_lo(pool, units[f"ffn{f}.up{c + 1}"], 1, it)

        step(0)
        step(1)
        step(2)
        with pool.Fori(0, TURNS) as it:
            step(3, it)
            step(4, it)
        step(9)
        for half in range(2):
            for j in range(3):
                split_lo(pool, units[f"ffn{f}.down{half}.{j}"], 1)
        for u in next_units:
            split_lo(pool, u, 1)
        reciprocal_rms(pool, FFN_NORM[f] + 1)

    S8 = NT * H1
    proj = cell("proj", 0, [P, 2, NT, 512])
    k_feat = cell("k_feat", 2, [P, H1, T])
    ya_hi = cell("ya_hi", 2, [P, 4, T], F32R)
    k_tok = cell("k_tok", 3, [P, NT, 512])
    state1 = cell("state1", 3, [P, 512])
    minus_wT = cell("minus_wT", 3, [P, 512], plus=2048)
    kn_feat = cell("kn_feat", 4, [P, H1, T])
    ya_lo = cell("ya_lo", 4, [P, 4, T], F32R)
    q_feat = cell("q_feat", 5, [P, H1, T])
    v_feat = cell("v_feat", 6, [P, H1, T])
    v_beta = cell("v_beta", 7, [P, NT, 512])
    low = cell("low", 8, [P, S8, P])
    o1 = cell("o1", 8, [P, NT, 512])
    attnT = cell("attnT", 9, [P, S8, P])
    lowT = cell("lowT", 10, [P, S8, P])
    inv = cell("inv", 11, [P, S8, P])
    invT = cell("invT", 12, [P, S8, P])
    corr = cell("corr", 13, [P, S8, P])
    o_state = cell("o_state", 13, [P, 512])
    z_act = cell("z_act", 14, [P, NT, 512])
    gm_v = cell("gm_v", 15, [P, NT, 512])
    gm_u = cell("gm_u", 16, [P, NT, 512])
    gm_wT = cell("gm_wT", 17, [P, GM_G, P])
    gm_rows = cell("gm_rows", 18, [P, 2, GM_W])
    k_beg = cell("k_beg", 19, [P, 512])
    k_dec = cell("k_dec", 19, [P, 512], plus=2048)
    v_new = cell("v_new", 20, [P, NT, 512])
    yb_hi = cell("yb_hi", 21, [P, 4, T], F32R)
    yb_lo = cell("yb_lo", 22, [P, 4, T], F32R)

    m1_conv = sb_small["m1_conv"]
    gm_bias = sb_small["gm_bias"]
    dn_rows = sb_small["dn_rows"]
    ba_raw, ba_hi, ba_lo, ba = (sb_small[k][:, :, :] for k in ("ba_raw", "ba_hi", "ba_lo", "ba"))
    sm = cell("sm", 23, [P, 17, NT * H1])
    level_mask = cell("level_mask", 21, [P, 8, P])
    below = cell("below", 22, [P, P])
    abs_a, soft, beta, log_g, neg_a, g_col, g_last = (sm[:, j, :] for j in range(7))
    exp_g, end_decay, k_ss, k_r, q_ss, q_r, o_ss, o_f, bexp, tanh_b = (sm[:, 7 + j, :] for j in range(10))
    by_t = "p (t h) -> p t h"

    S = Signals(nc, ctx)
    ONCE = {
      "pe": (
        "ba_done", "k_proj_t", "g_sums", "k_tok_t", "q_proj_t", "kn_t", "g_rows", "gram_done", "v_proj_t",
        "lowT_t", "v_tok_t", "scores_done", "q_tok_t", "gm_mixed", "ya_t", "v_new0_product", "wT_product",
        "state_product", "v_new1_product", "yb_t", "dt_done", "B_tok_t", "dt_sums", "cb_done"),
      "act": (
        "ba_rounded", "a_ready", "ba_scaled", "tanh_ready", "ln_ready", "k_feat_ready", "k_squared",
        "q_feat_ready", "decay_exp", "decayT_exp", "exp_g_ready", "v_feat_ready", "q_squared",
        "dt_rounded", "a2_ready", "dt_ln", "B_tok_ready", "mem_squared"),
      "dve": (
        "ba_split", "a_biased", "k_conv_done", "log_g_ready", "row_ready", "g_read", "q_conv_done",
        "k_tok_ready", "g_rows_read", "diff_ready", "v_conv_done", "gm_stats", "dt_split", "dt_biased",
        "la_ready", "w_end_in", "dt_ready", "w_end_ready"),
    }
    STEP = {name: (engine, n + 1) for engine, names in ONCE.items() for n, name in enumerate(names)}
    steps_made = {engine: 0 for engine in ONCE}

    def once(name):
        return S[STEP[name][0] + "_steps"], STEP[name][1]

    def step(name):
        engine, n = STEP[name]
        steps_made[engine] += 1
        assert steps_made[engine] == n, f"{name} is out of order"
        return S[engine + "_steps"]

    dve_count = [0]

    def dlink(op):
        op.then_inc(S["dve_chain"], 1)
        dve_count[0] += 1
        return dve_count[0]

    def dwait(dve, n=None):
        dve.wait_ge(S["dve_chain"], dve_count[0] if n is None else n)

    act_count = [0]

    def alink(op):
        op.then_inc(S["act_chain"], 1)
        act_count[0] += 1

    def await_own(act):
        act.wait_ge(S["act_chain"], act_count[0])

    def plink(op):
        op.then_inc(pool_chain, 1)
        chained[0] += 1

    def pwait(pool):
        pool.wait_ge(pool_chain, chained[0])

    def flat(a):
        return a.rearrange("p a b -> p (a b)")

    def bank(n, k=1):
        return work[:, n, :] if k == 1 else work[:, n:n + k, :].rearrange("p a b -> p (a b)")

    def to_features(pe, src, n):
        for blk in range(4):
            for t in range(NT):
                tr = pe.transpose(work[:, n + blk // 2, (blk % 2) * T + t * P:(blk % 2) * T + (t + 1) * P],
                                  src[:, t, blk * P:(blk + 1) * P], ident[:, :])
        return tr

    def to_tokens(pe, src, n):
        for t in range(NT):
            for blk in range(4):
                tr = pe.transpose(work[:, n + t, blk * P:(blk + 1) * P], src[:, blk, t * P:(t + 1) * P],
                                  ident[:, :])
        return tr

    def feature_block(n, blk):
        return work[:, n + blk // 2, (blk % 2) * T:(blk % 2 + 1) * T]

    def conv(dve, n, dst, taps, weight):
        last = [dlink(dve.tensor_scalar(dst[:, blk, :], feature_block(n, blk), weight(blk, taps - 1), None,
                                        ALU.mult)) for blk in range(4)]
        for s in range(1, taps):
            for blk in range(4):
                dwait(dve, last[blk])
                last[blk] = dlink(dve.scalar_tensor_tensor(
                    out=dst[:, blk, s:T], in0=feature_block(n, blk)[:, 0:T - s],
                    scalar=weight(blk, taps - 1 - s), in1=dst[:, blk, s:T], op0=ALU.mult, op1=ALU.add))

    def m1_loads(sp):
        for j, name in enumerate(("k", "q", "v", "gv", "gu", "z")):
            for i in range(2):
                load(sp, units["m1." + name], i, w["t_m1_in"][(3, 2, 4, 1, 0, 5)[j]])
        for name in ("out_a", "out_b"):
            for i in range(2):
                load(sp, units["m1." + name], i, w["t_m1_out"][i])

    def narrow(pe, hi, lo, n, dst):
        for t in range(NT):
            tok = slice(t * P, (t + 1) * P)
            for kt in range(KD):
                pe.matmul(dst(t), xT_hi[:, kt, tok], hi[:, kt, :], start=kt == 0, stop=False)
                pe.matmul(dst(t), xT_hi[:, kt, tok], lo[:, kt, :], start=False, stop=False)
                mm = pe.matmul(dst(t), xT_lo[:, kt, tok], hi[:, kt, :], start=False, stop=kt == KD - 1)
        return mm

    def m1_banks(j):
        return pair((j + 1) % 2)

    def per_head(pe, t, lhsT, rhs, n):
        for h in range(H1):
            mm = pe.matmul(work[:, n, h * P:(h + 1) * P], lhsT(h), rhs(h), start=True, stop=True)
        return mm

    def level_products(pe, level, part):
        for t in range(NT):
            n = H1 * t
            if part == 0:
                pe.wait_ge(S["inv_ready"], NT * (level - 1) + t + 1)
                pe.wait_ge(S["invT_ready"], NT * (level - 1) + t + 1)
                mm = per_head(pe, t, lambda h: lowT[:, n + h, :], lambda h: inv[:, n + h, :], 2 + t)
                mm.then_inc(S["corr_product"], 1)
            elif part == 1:
                pe.wait_ge(S["corr_ready"], NT * (level - 1) + t + 1)
                if level < LEVELS - 1:
                    mm = per_head(pe, t, lambda h: invT[:, n + h, :], lambda h: corr[:, n + h, :], 2 + t)
                    mm.then_inc(S["inv_product"], 1)
            else:
                if level < LEVELS - 1:
                    pe.wait_ge(S["inv_ready"], NT * level + t + 1)
                mm = per_head(pe, t, lambda h: corr[:, n + h, :], lambda h: invT[:, n + h, :], 2 + t)
                mm.then_inc(S["invT_product"], 1)

    def level_updates(dve, level, part):
        mask = level_mask[:, level, :].rearrange("p (a b) -> p a b", a=1).broadcast_to([P, H1, P])
        for t in range(NT):
            n = slice(H1 * t, H1 * t + H1)
            product = work[:, 2 + t, :].rearrange("p (h b) -> p h b", h=H1)
            if part == 0:
                dve.wait_ge(S["corr_product"], NT * (level - 1) + t + 1)
                dve.tensor_tensor(corr[:, n, :], product, mask, ALU.mult).then_inc(S["corr_ready"], 1)
            elif part == 1 and level < LEVELS - 1:
                dve.wait_ge(S["inv_product"], NT * (level - 1) + t + 1)
                dve.tensor_tensor(inv[:, n, :], inv[:, n, :], product, ALU.subtract).then_inc(S["inv_ready"], 1)
            elif part == 2:
                dve.wait_ge(S["invT_product"], NT * (level - 1) + t + 1)
                dve.tensor_tensor(invT[:, n, :], invT[:, n, :], product, ALU.subtract).then_inc(S["invT_ready"], 1)

    LEVELS = len(SOLVE_LEVELS)
    STEPS = [(level, part) for level in range(1, LEVELS) for part in range(3)]

    def m1_tensor(pe):
        at = {}

        def run(name, j, pre=None):
            if pre is not None:
                pre()
            u = units["m1." + name]
            for i in range(2):
                sides = {k: at[(name, i, k)] for k in range(4) if (name, i, k) in at}
                if name == "k":
                    pe.wait_ge(xlo_done, 2 * B_MIX1 + i + 1)
                multiply(pe, u, i, xT_hi, xT_lo, m1_banks(j), i == 0, i == 1, None, sides)

        def k_features():
            pe.wait_ge(S["proj_ready"], 2)
            to_features(pe, proj[:, 0, :, :], 0).then_inc(step("k_proj_t"), 1)

        def decay_sums():
            pe.wait_ge(*once("log_g_ready"))
            pe.matmul(work[:, 3, 32:40], up_to[:, :], log_g, start=True, stop=True)
            pe.matmul(work[:, 3, 40:48], ones[:, :], log_g, start=True, stop=True).then_inc(step("g_sums"), 1)

        def k_tokens():
            pe.wait_ge(*once("k_feat_ready"))
            pe.wait_ge(*once("g_read"))
            to_tokens(pe, k_feat, 2).then_inc(step("k_tok_t"), 1)

        def q_features():
            pe.wait_ge(S["proj_ready"], 4)
            pe.wait_ge(*once("k_conv_done"))
            to_features(pe, proj[:, 1, :, :], 0).then_inc(step("q_proj_t"), 1)

        def decay_rows():
            pe.wait_ge(*once("row_ready"))
            pe.wait_ge(*once("q_conv_done"))
            pe.matmul(work[:, 0, :], ones[:, :], flat(lowT[:, 0:H1, :]), start=True, stop=True)
            pe.matmul(work[:, 1, :], ones[:, :], flat(lowT[:, H1:S8, :]), start=True,
                      stop=True).then_inc(step("g_rows"), 1)

        def kn_features():
            pe.wait_ge(*once("k_tok_ready"))
            to_features(pe, k_tok, 2).then_inc(step("kn_t"), 1)

        def gram():
            pe.wait_ge(S["kn_feat_ready"], 2)
            for t in range(NT):
                tok = slice(t * P, (t + 1) * P)
                mm = per_head(pe, t, lambda h: kn_feat[:, h, tok], lambda h: kn_feat[:, h, tok], 2 + t)
            mm.then_inc(step("gram_done"), 1)

        def v_features():
            pe.wait_ge(S["proj_ready"], 6)
            pe.wait_ge(*once("g_rows_read"))
            to_features(pe, proj[:, 0, :, :], 0).then_inc(step("v_proj_t"), 1)

        def low_transposed():
            pe.wait_ge(S["low_ready"], NT)
            for n in range(S8):
                tr = pe.transpose(work[:, 2 + n // H1, (n % H1) * P:(n % H1 + 1) * P], low[:, n, :], ident[:, :])
            tr.then_inc(step("lowT_t"), 1)

        def v_tokens():
            pe.wait_ge(*once("v_feat_ready"))
            to_tokens(pe, v_feat, 0).then_inc(step("v_tok_t"), 1)

        def scores():
            pe.wait_ge(S["v_beta_ready"], NT)
            for t in range(NT):
                tok = slice(t * P, (t + 1) * P)
                mm = per_head(pe, t, lambda h: kn_feat[:, h, tok], lambda h: q_feat[:, h, tok], t)
            mm.then_inc(step("scores_done"), 1)

        def q_tokens():
            pe.wait_ge(S["attnT_ready"], NT)
            to_tokens(pe, q_feat, 0).then_inc(step("q_tok_t"), 1)

        def gm_mix():
            pe.wait_ge(S["gm_norm_ready"], NT)
            pe.wait_ge(S["gm_masked"], 1)
            pe.wait_ge(*once("q_squared"))
            for t in range(NT):
                for g in range(GM_G):
                    c = slice(g * GM_C, (g + 1) * GM_C)
                    mm = pe.matmul(work[:, t, c], gm_wT[:, g, :], gm_v[:, t, c], start=True, stop=True)
            mm.then_inc(step("gm_mixed"), 1)

        def ya_features():
            pe.wait_ge(S["ya_ready"], NT)
            to_features(pe, gm_u, 0).then_inc(step("ya_t"), 1)

        tok1 = slice(P, 2 * P)

        def chain1():
            pe.wait_ge(S["invT_ready"], NT * LEVELS)
            pe.wait_ge(S["ya_split"], 2)
            pe.wait_ge(S["k_scaled"], 1)
            per_head(pe, 0, lambda h: invT[:, h, :], lambda h: v_beta[:, 0, h * P:(h + 1) * P],
                     0).then_inc(step("v_new0_product"), 1)
            per_head(pe, 1, lambda h: k_beg[:, h * P:(h + 1) * P], lambda h: invT[:, H1 + h, :],
                     1).then_inc(step("wT_product"), 1)

        def chain2():
            pe.wait_ge(S["v_new_ready"], 1)
            per_head(pe, 0, lambda h: k_dec[:, h * P:(h + 1) * P], lambda h: v_new[:, 0, h * P:(h + 1) * P],
                     2).then_inc(step("state_product"), 1)
            per_head(pe, 0, lambda h: attnT[:, h, :], lambda h: v_new[:, 0, h * P:(h + 1) * P],
                     0).then_inc(S["o_products"], 1)

        def chain3():
            pe.wait_ge(S["state_ready"], 2)
            for h in range(H1):
                c = slice(h * P, (h + 1) * P)
                pe.matmul(work[:, 3, c], invT[:, H1 + h, :], v_beta[:, 1, c], start=True, stop=False)
                mm = pe.matmul(work[:, 3, c], minus_wT[:, c], state1[:, c], start=False, stop=True)
            mm.then_inc(step("v_new1_product"), 1)
            per_head(pe, 1, lambda h: q_feat[:, h, tok1], lambda h: state1[:, h * P:(h + 1) * P],
                     1).then_inc(S["o_products"], 1)

        def chain4():
            pe.wait_ge(S["v_new_ready"], 2)
            per_head(pe, 1, lambda h: attnT[:, H1 + h, :], lambda h: v_new[:, 1, h * P:(h + 1) * P],
                     2).then_inc(S["o_products"], 1)

        def yb_features():
            pe.wait_ge(S["yb_ready"], NT)
            to_features(pe, o1, 0).then_inc(step("yb_t"), 1)

        at[("k", 0, 1)] = lambda: transpose_x(pe, B_MIX1, 1)
        at[("q", 0, 0)] = k_features
        at[("q", 1, 1)] = decay_sums
        at[("q", 1, 3)] = k_tokens
        at[("v", 0, 1)] = q_features
        at[("v", 1, 1)] = kn_features
        at[("v", 1, 2)] = decay_rows
        at[("gv", 0, 0)] = gram
        at[("gv", 0, 1)] = v_features
        at[("gv", 1, 1)] = low_transposed
        at[("gv", 1, 3)] = v_tokens

        def both(a, b):
            def run_both():
                a()
                b()
            return run_both

        spots = [(n, i, k) for n in ("gu", "z", "out_a") for i in range(2) for k in range(4)]
        for spot, (level, part) in zip(spots[1:], STEPS):
            at[spot] = lambda level=level, part=part: level_products(pe, level, part)
        for spot, side in ((("gu", 0, 1), scores), (("gu", 1, 0), q_tokens), (("z", 0, 3), gm_mix),
                           (("z", 1, 3), ya_features)):
            at[spot] = both(side, at[spot])
        for spot, side in zip(spots[1 + len(STEPS):], (chain1, chain2, chain3, chain4)):
            at[spot] = side

        run("k", 0)
        pe.wait_ge(*once("ba_split"))
        narrow(pe, ba_hi, ba_lo, 8, lambda t: work[:, 3, 8 * t:8 * t + 8]).then_inc(step("ba_done"), 1)
        run("q", 1)
        run("v", 2, lambda: pe.wait_ge(S["acc_read"], 1))
        run("gv", 3, lambda: pe.wait_ge(S["acc_read"], 2))
        run("gu", 4, lambda: pe.wait_ge(S["acc_read"], 3))
        run("z", 5, lambda: pe.wait_ge(S["acc_read"], 4))
        ua, ub = units["m1.out_a"], units["m1.out_b"]
        pe.wait_ge(S["ya_split"], 2)
        pe.wait_ge(S["acc_read"], 5)
        multiply(pe, ua, 0, ya_hi, ya_lo, pair(1), True, False, None, {k: at[("out_a", 0, k)] for k in range(4) if ("out_a", 0, k) in at})
        pe.wait_ge(S["acc_read"], 6)
        multiply(pe, ua, 1, ya_hi, ya_lo, pair(0), True, False, None, {k: at[("out_a", 1, k)] for k in range(4) if ("out_a", 1, k) in at})
        yb_features()
        pe.wait_ge(S["yb_split"], 2)
        multiply(pe, ub, 0, yb_hi, yb_lo, pair(1), False, True, k0=4)
        multiply(pe, ub, 1, yb_hi, yb_lo, pair(0), False, True, None, {1: lambda: transpose_x(pe, B_FFN1, 0)}, k0=4)

    def m1_scalar(act):
        b = B_MIX1
        sides = []

        def evac(name, j, dst, func=ACT.Copy, signal=None):
            wait_unit_done(act, units["m1." + name])
            for t in range(NT):
                act.activation(dst[:, t, :], m1_banks(j)[t], func, scale=rstd[:, t:t + 1]).then_inc(signal, 1)
            act.wait_ge(signal, evac.counts.setdefault(id(signal), 0) + NT)
            evac.counts[id(signal)] += NT
            act.sem_inc(S["acc_read"], 1)
        evac.counts = {}

        def splits(name):
            split_hi(act, units["m1." + name], 0)
            split_hi(act, units["m1." + name], 1)

        round_xt(act, b, 1)
        act.activation(ba_hi, ba_raw, ACT.Copy).then_inc(step("ba_rounded"), 1)
        alink(act.activation(neg_a[:, 0:H1], dn_rows[:, 1, :], ACT.Exp))
        alink(act.activation(neg_a[:, H1:2 * H1], dn_rows[:, 1, :], ACT.Exp))
        await_own(act)
        act.sem_inc(step("a_ready"), 1)
        splits("q")
        act.wait_ge(rstd_ready, b + 1)
        evac("k", 0, proj[:, 0, :, :], signal=S["proj_ready"])
        act.wait_ge(*once("ba_done"))
        for t in range(NT):
            alink(act.activation(ba[:, t, :], work[:, 3, 8 * t:8 * t + 8], ACT.Copy, scale=rstd[:, t:t + 1]))
        await_own(act)
        act.sem_inc(step("ba_scaled"), 1)
        split_hi(act, units["m1.v"], 0)
        act.activation(tanh_b.rearrange(by_t, t=NT), ba[:, :, 0:H1], ACT.Tanh, scale=0.5).then_inc(step("tanh_ready"), 1)
        act.wait_ge(*once("a_biased"))
        alink(act.activation(abs_a, soft, ACT.Abs))
        await_own(act)
        alink(act.activation(abs_a, abs_a, ACT.Exp, scale=-1.0))
        await_own(act)
        act.activation(abs_a, abs_a, ACT.Ln, bias=1.0).then_inc(step("ln_ready"), 1)
        act.wait_ge(*once("k_conv_done"))
        act.activation(flat(k_feat), flat(k_feat), ACT.Silu).then_inc(step("k_feat_ready"), 1)
        split_hi(act, units["m1.v"], 1)
        evac("q", 1, proj[:, 1, :, :], signal=S["proj_ready"])
        split_hi(act, units["m1.gv"], 0)
        act.wait_ge(*once("k_tok_t"))
        for n in range(S8):
            square(act, work[:, 2 + n // H1, (n % H1) * P:(n % H1 + 1) * P], k_ss[:, n:n + 1])
        act.wait_ge(squares, squared[0])
        act.sem_inc(step("k_squared"), 1)
        split_hi(act, units["m1.gv"], 1)
        act.wait_ge(*once("kn_t"))
        for j in range(2):
            act.activation(flat(kn_feat[:, 2 * j:2 * j + 2, :]), bank(2 + j), ACT.Copy).then_inc(S["kn_feat_ready"], 1)
        act.wait_ge(*once("q_conv_done"))
        act.activation(flat(q_feat), flat(q_feat), ACT.Silu).then_inc(step("q_feat_ready"), 1)
        evac("v", 2, proj[:, 0, :, :], signal=S["proj_ready"])
        act.wait_ge(*once("diff_ready"))
        act.activation(flat(low), flat(low), ACT.Exp).then_inc(step("decay_exp"), 1)
        act.activation(flat(attnT), flat(attnT), ACT.Exp).then_inc(step("decayT_exp"), 1)
        act.wait_ge(*once("g_read"))
        alink(act.activation(exp_g, g_col, ACT.Exp))
        act.activation(end_decay, end_decay, ACT.Exp).then_inc(step("exp_g_ready"), 1)
        split_hi(act, units["m1.gu"], 0)
        act.wait_ge(*once("lowT_t"))
        for t in range(NT):
            act.activation(flat(lowT[:, H1 * t:H1 * t + H1, :]), bank(2 + t), ACT.Copy).then_inc(S["lowT_ready"], 1)
        act.wait_ge(*once("v_conv_done"))
        act.activation(flat(v_feat), flat(v_feat), ACT.Silu).then_inc(step("v_feat_ready"), 1)
        split_hi(act, units["m1.gu"], 1)
        evac("gv", 3, gm_v, ACT.Gelu_apprx_tanh, S["gm_v_ready"])
        split_hi(act, units["m1.z"], 0)
        act.wait_ge(*once("q_tok_t"))
        for n in range(S8):
            square(act, work[:, n // H1, (n % H1) * P:(n % H1 + 1) * P], q_ss[:, n:n + 1])
        act.wait_ge(squares, squared[0])
        act.sem_inc(step("q_squared"), 1)
        split_hi(act, units["m1.z"], 1)
        evac("gu", 4, gm_u, ACT.Gelu_apprx_tanh, S["gm_u_ready"])
        split_hi(act, units["m1.out_a"], 0)
        split_hi(act, units["m1.out_a"], 1)
        act.wait_ge(*once("ya_t"))
        for j in range(2):
            act.activation(flat(ya_hi[:, 2 * j:2 * j + 2, :]), bank(j), ACT.Copy).then_inc(S["ya_rounded"], 1)
        evac("z", 5, z_act, ACT.Silu, S["z_ready"])
        split_hi(act, units["m1.out_b"], 0)
        act.wait_ge(*once("v_new0_product"))
        act.activation(v_new[:, 0, :], bank(0), ACT.Copy).then_inc(S["v_new_ready"], 1)
        act.wait_ge(*once("wT_product"))
        act.activation(minus_wT[:, :], bank(1), ACT.Copy, scale=-1.0).then_inc(S["state_ready"], 1)
        act.wait_ge(*once("state_product"))
        act.activation(state1[:, :], bank(2), ACT.Copy).then_inc(S["state_ready"], 1)
        split_hi(act, units["m1.out_b"], 1)
        act.wait_ge(*once("v_new1_product"))
        act.activation(v_new[:, 1, :], bank(3), ACT.Copy).then_inc(S["v_new_ready"], 1)
        for t in range(NT):
            act.wait_ge(S["o_raw"], t + 1)
            for h in range(H1):
                n = H1 * t + h
                square(act, o1[:, t, h * P:(h + 1) * P], o_ss[:, n:n + 1])
            act.wait_ge(squares, squared[0])
            act.sem_inc(S["o_squared"], 1)
        u = units["ffn1.up0"]
        split_hi(act, u, 0)
        act.wait_ge(*once("yb_t"))
        for j in range(2):
            act.activation(flat(yb_hi[:, 2 * j:2 * j + 2, :]), bank(j), ACT.Copy,
                           scale=dn_gain[:, :]).then_inc(S["yb_rounded"], 1)
        square_x(act, B_FFN1, 0)
        round_xt(act, B_FFN1, 0)
        split_hi(act, u, 1)
        square_x(act, B_FFN1, 1)
        act.dma_start(gfinal_row[:, :], w["r_final"][0:1, :].broadcast_to([P, D])).then_inc(final1_loaded, 16)

    def m1_vector(dve):
        b = B_MIX1
        wt = lambda base: (lambda blk, tap: m1_conv[:, base + blk, tap:tap + 1])
        heads = "p (h d) -> p h d"

        def over_d(v):
            return v.rearrange("p (h a) -> p h a", a=1).broadcast_to([P, v.shape[-1], P])

        rest_xt(dve, b, 1)
        dve.wait_ge(*once("ba_rounded"))
        dve.tensor_tensor(ba_lo, ba_raw, ba_hi.bitcast(F32), ALU.subtract).then_inc(step("ba_split"), 1)
        split_lo(dve, units["m1.q"], 0)
        dve.wait_ge(*once("ba_scaled"))
        for t in range(NT):
            dlink(dve.tensor_tensor(soft[:, H1 * t:H1 * t + H1], ba[:, t, H1:2 * H1], dn_rows[:, 0, :], ALU.add))
        dwait(dve)
        dve.sem_inc(step("a_biased"), 1)
        dve.wait_ge(*once("k_proj_t"))
        split_lo(dve, units["m1.v"], 0)
        conv(dve, 0, k_feat, TAPS1, wt(4))
        dwait(dve)
        dve.sem_inc(step("k_conv_done"), 1)
        dve.wait_ge(*once("tanh_ready"))
        dlink(dve.tensor_scalar(beta, tanh_b, 0.5, 0.5, ALU.mult, ALU.add))
        dve.wait_ge(*once("ln_ready"))
        dwait(dve)
        dlink(dve.scalar_tensor_tensor(out=soft, in0=soft, scalar=0.0, in1=abs_a, op0=ALU.max, op1=ALU.add))
        dve.wait_ge(*once("a_ready"))
        dwait(dve)
        dlink(dve.scalar_tensor_tensor(out=log_g, in0=soft, scalar=-1.0, in1=neg_a, op0=ALU.mult, op1=ALU.mult))
        dwait(dve)
        dve.sem_inc(step("log_g_ready"), 1)
        tri = up_to[:, :].rearrange("p (a b) -> p a b", a=1).broadcast_to([P, S8, P])
        dve.tensor_tensor(lowT[:, :, :], tri, over_d(log_g), ALU.mult).then_inc(step("row_ready"), 1)
        dve.wait_ge(*once("g_sums"))
        dlink(dve.tensor_copy(g_col, work[:, 3, 32:40]))
        dlink(dve.tensor_copy(g_last, work[:, 3, 40:48]))
        dwait(dve)
        dlink(dve.tensor_tensor(end_decay, g_last, g_col, ALU.subtract))
        dwait(dve)
        dve.sem_inc(step("g_read"), 1)
        split_lo(dve, units["m1.gv"], 0)
        dve.wait_ge(*once("q_proj_t"))
        conv(dve, 0, q_feat, TAPS1, wt(0))
        dwait(dve)
        dve.sem_inc(step("q_conv_done"), 1)
        dve.wait_ge(S["k_scale_ready"], 1)
        for t in range(NT):
            dlink(dve.tensor_tensor(k_tok[:, t, :].rearrange(heads, h=H1), work[:, 2 + t, :].rearrange(heads, h=H1),
                                    over_d(k_r[:, H1 * t:H1 * t + H1]), ALU.mult))
        dwait(dve)
        dve.sem_inc(step("k_tok_ready"), 1)
        dve.wait_ge(*once("g_rows"))
        for t in range(NT):
            n = slice(H1 * t, H1 * t + H1)
            dlink(dve.tensor_tensor(low[:, n, :], over_d(g_col[:, n]),
                                    work[:, t, :].rearrange(heads, h=H1), ALU.subtract))
        dwait(dve)
        dve.sem_inc(step("g_rows_read"), 1)
        dlink(dve.tensor_scalar(flat(attnT), flat(low), -1.0, 0.0, ALU.mult, ALU.min))
        dwait(dve)
        dlink(dve.tensor_scalar(flat(low), flat(low), 0.0, None, ALU.min))
        dwait(dve)
        dve.sem_inc(step("diff_ready"), 1)
        dve.wait_ge(*once("decay_exp"))
        for n in range(S8):
            dlink(dve.scalar_tensor_tensor(out=low[:, n, :], in0=low[:, n, :], scalar=beta[:, n:n + 1],
                                           in1=below[:, :], op0=ALU.mult, op1=ALU.mult))
        dwait(dve)
        dve.wait_ge(*once("gram_done"))
        for t in range(NT):
            n = slice(H1 * t, H1 * t + H1)
            dve.tensor_tensor(flat(low[:, n, :]), flat(low[:, n, :]), bank(2 + t), ALU.mult).then_inc(S["low_ready"], 1)
        split_lo(dve, units["m1.gu"], 0)
        dve.wait_ge(*once("v_proj_t"))
        conv(dve, 0, v_feat, TAPS1, wt(8))
        dwait(dve)
        dve.sem_inc(step("v_conv_done"), 1)
        eye = ident[:, :].rearrange("p (a b) -> p a b", a=1).broadcast_to([P, H1, P])
        for t in range(NT):
            n = slice(H1 * t, H1 * t + H1)
            dve.wait_ge(S["level0_masked"], t + 1)
            dve.tensor_tensor(inv[:, n, :], eye, inv[:, n, :], ALU.subtract).then_inc(S["inv_ready"], 1)
        for t in range(NT):
            n = slice(H1 * t, H1 * t + H1)
            dve.wait_ge(S["level0_masked"], NT + t + 1)
            dve.tensor_tensor(invT[:, n, :], eye, invT[:, n, :], ALU.subtract).then_inc(S["invT_ready"], 1)
        dve.wait_ge(*once("v_tok_t"))
        for t in range(NT):
            dve.tensor_tensor(v_beta[:, t, :].rearrange(heads, h=H1), bank(t).rearrange(heads, h=H1),
                              over_d(beta[:, H1 * t:H1 * t + H1]), ALU.mult).then_inc(S["v_beta_ready"], 1)
        split_lo(dve, units["m1.z"], 0)
        steps = iter(STEPS)

        def level_steps(k):
            for _ in range(k):
                level_updates(dve, *next(steps))

        level_steps(1)
        dve.wait_ge(S["decayT_masked"], 1)
        dve.wait_ge(*once("scores_done"))
        for t in range(NT):
            n = slice(H1 * t, H1 * t + H1)
            dve.tensor_tensor(flat(attnT[:, n, :]), flat(attnT[:, n, :]), bank(t), ALU.mult).then_inc(S["attnT_ready"], 1)
        level_steps(6)
        split_lo(dve, units["m1.out_a"], 0)
        stats, mv = sb_small["stats"], sb_small["mv"]
        dve.wait_ge(S["gm_v_ready"], NT)
        for t in range(NT):
            dlink(dve.bn_stats(stats[:, t, :], gm_v[:, t, :]))
        dwait(dve)
        for t in range(NT):
            dlink(dve.bn_aggr(mv[:, t, :], stats[:, t, :]))
        dwait(dve)
        dve.sem_inc(step("gm_stats"), 1)
        level_steps(1)
        dve.wait_ge(S["gm_rstd"], 1)
        for t in range(NT):
            dlink(dve.tensor_scalar(gm_v[:, t, :], gm_v[:, t, :], mv[:, t, 0:1], gm_r[:, t:t + 1],
                                    ALU.subtract, ALU.mult))
        dwait(dve)
        for t in range(NT):
            dlink(dve.tensor_tensor(gm_v[:, t, :], gm_v[:, t, :], gm_rows[:, 0, :], ALU.mult))
        dwait(dve)
        for t in range(NT):
            dve.tensor_tensor(gm_v[:, t, :], gm_v[:, t, :], gm_rows[:, 1, :], ALU.add).then_inc(S["gm_norm_ready"], 1)
        level_steps(3)
        bias = gm_bias[:, :].rearrange("p (g a) -> p g a", a=1).broadcast_to([P, GM_G, GM_C])
        groups = "p (g c) -> p g c"
        dve.wait_ge(*once("gm_mixed"))
        for t in range(NT):
            dlink(dve.tensor_tensor(gm_v[:, t, :].rearrange(groups, g=GM_G), bank(t).rearrange(groups, g=GM_G),
                                    bias, ALU.add))
        dwait(dve)
        dve.wait_ge(S["gm_u_ready"], NT)
        for t in range(NT):
            dve.tensor_tensor(gm_u[:, t, :], gm_u[:, t, :], gm_v[:, t, :], ALU.mult).then_inc(S["ya_ready"], 1)
        level_steps(4)
        for j in range(2):
            dve.wait_ge(S["ya_rounded"], j + 1)
            dve.tensor_tensor(flat(ya_lo[:, 2 * j:2 * j + 2, :]), bank(j),
                              flat(ya_hi[:, 2 * j:2 * j + 2, :]).bitcast(F32), ALU.subtract).then_inc(S["ya_split"], 1)
        split_lo(dve, units["m1.out_b"], 0)
        level_steps(3)
        dve.wait_ge(S["o_products"], 1)
        dve.tensor_copy(o1[:, 0, :], bank(0)).then_inc(S["o_raw"], 1)
        dve.wait_ge(S["o_products"], 2)
        dlink(dve.tensor_tensor(o_state[:, :].rearrange(heads, h=H1), bank(1).rearrange(heads, h=H1),
                                over_d(exp_g[:, H1:2 * H1]), ALU.mult))
        dwait(dve)
        dve.wait_ge(S["o_products"], 3)
        dve.tensor_tensor(o1[:, 1, :], o_state[:, :], bank(2), ALU.add).then_inc(S["o_raw"], 1)
        split_lo(dve, units["ffn1.up0"], 0)
        dve.wait_ge(S["z_ready"], NT)
        dve.wait_ge(S["o_scale_ready"], 1)
        for t in range(NT):
            o_t = o1[:, t, :].rearrange(heads, h=H1)
            dlink(dve.tensor_tensor(o_t, o_t, over_d(o_f[:, H1 * t:H1 * t + H1]), ALU.mult))
        dwait(dve)
        for t in range(NT):
            dve.tensor_tensor(o1[:, t, :], o1[:, t, :], z_act[:, t, :], ALU.mult).then_inc(S["yb_ready"], 1)
        for j in range(2):
            dve.wait_ge(S["yb_rounded"], j + 1)
            dve.scalar_tensor_tensor(out=flat(yb_lo[:, 2 * j:2 * j + 2, :]), in0=bank(j), scalar=dn_gain[:, :],
                                     in1=flat(yb_hi[:, 2 * j:2 * j + 2, :]).bitcast(F32), op0=ALU.mult,
                                     op1=ALU.subtract).then_inc(S["yb_split"], 1)
        residual_half(dve, B_FFN1, 0, units["m1.out_b"].g + 1, pair(1), 1.0)
        rest_xt(dve, B_FFN1, 0)
        residual_half(dve, B_FFN1, 1, units["m1.out_b"].g + 2, pair(0), 1.0)

    def m1_pool(pool):
        def over_d(v):
            return v.rearrange("p (h a) -> p h a", a=1).broadcast_to([P, v.shape[-1], P])

        heads = "p (h d) -> p h d"
        scale2 = 1.0 / DH1
        split_lo(pool, units["m1.q"], 1)
        split_lo(pool, units["m1.v"], 1)
        pool.wait_ge(*once("k_squared"))
        plink(pool.tensor_scalar(k_ss, k_ss, EPS, None, ALU.add))
        pwait(pool)
        plink(pool.tensor_tensor(k_r, k_ss, minus_half[:, 0:S8], ALU.pow))
        pwait(pool)
        pool.sem_inc(S["k_scale_ready"], 1)
        split_lo(pool, units["m1.gv"], 1)
        pool.wait_ge(consts_loaded, 16 * N_CONSTS)
        pool.wait_ge(*once("decayT_exp"))
        tri = up_to[:, :].rearrange("p (a b) -> p a b", a=1).broadcast_to([P, S8, P])
        pool.tensor_tensor(attnT[:, :, :], attnT[:, :, :], tri, ALU.mult).then_inc(S["decayT_masked"], 1)
        m0 = level_mask[:, 0, :].rearrange("p (a b) -> p a b", a=1).broadcast_to([P, H1, P])
        m0T = level_mask[:, 7, :].rearrange("p (a b) -> p a b", a=1).broadcast_to([P, H1, P])
        for t in range(NT):
            n = slice(H1 * t, H1 * t + H1)
            pool.wait_ge(S["low_ready"], t + 1)
            pool.tensor_tensor(inv[:, n, :], low[:, n, :], m0, ALU.mult).then_inc(S["level0_masked"], 1)
        for t in range(NT):
            n = slice(H1 * t, H1 * t + H1)
            pool.wait_ge(S["lowT_ready"], t + 1)
            pool.tensor_tensor(invT[:, n, :], lowT[:, n, :], m0T, ALU.mult).then_inc(S["level0_masked"], 1)
        split_lo(pool, units["m1.gu"], 1)
        pool.wait_ge(*once("exp_g_ready"))
        plink(pool.tensor_tensor(bexp, beta, exp_g, ALU.mult))
        pwait(pool)
        plink(pool.tensor_tensor(k_beg[:, :].rearrange(heads, h=H1), k_tok[:, 1, :].rearrange(heads, h=H1),
                                 over_d(bexp[:, H1:2 * H1]), ALU.mult))
        plink(pool.tensor_tensor(k_dec[:, :].rearrange(heads, h=H1), k_tok[:, 0, :].rearrange(heads, h=H1),
                                 over_d(end_decay[:, 0:H1]), ALU.mult))
        pwait(pool)
        pool.sem_inc(S["k_scaled"], 1)
        split_lo(pool, units["m1.z"], 1)
        pool.wait_ge(*once("q_squared"))
        plink(pool.tensor_scalar(q_ss, q_ss, EPS, None, ALU.add))
        pool.wait_ge(*once("gm_stats"))
        plink(pool.tensor_scalar(gm_r[:, :], sb_small["mv"][:, :, 1], EPS, None, ALU.add))
        pwait(pool)
        plink(pool.tensor_tensor(gm_r[:, :], gm_r[:, :], minus_half[:, 0:NT], ALU.pow))
        pwait(pool)
        pool.sem_inc(S["gm_rstd"], 1)
        plink(pool.tensor_tensor(q_r, q_ss, minus_half[:, 0:S8], ALU.pow))
        split_lo(pool, units["m1.out_a"], 1)
        split_lo(pool, units["m1.out_b"], 1)
        pool.wait_ge(S["o_squared"], NT)
        plink(pool.tensor_tensor(o_f, q_r, q_r, ALU.mult))
        pwait(pool)
        plink(pool.tensor_tensor(o_f, o_f, o_ss, ALU.mult))
        pwait(pool)
        plink(pool.tensor_scalar(o_f, o_f, scale2 / DH1, EPS, ALU.mult, ALU.add))
        pwait(pool)
        plink(pool.tensor_tensor(o_f, o_f, minus_half[:, 0:S8], ALU.pow))
        pwait(pool)
        plink(pool.tensor_tensor(o_f, o_f, q_r, ALU.mult))
        pwait(pool)
        plink(pool.tensor_scalar(o_f, o_f, DH1 ** -0.5, None, ALU.mult))
        pwait(pool)
        pool.sem_inc(S["o_scale_ready"], 1)
        split_lo(pool, units["ffn1.up0"], 1)
        reciprocal_rms(pool, B_FFN1)

    HALF = 512
    B_feat = cell("B_feat", 2, [P, SSM_G, T])
    C_feat = cell("C_feat", 3, [P, SSM_G, T])
    B_tok0 = cell("B_tok0", 4, [P, SSM_G * P])
    state0 = cell("state0", 4, [P, 512], plus=2048)
    x_tok = [cell(f"x_tok{g}", 5 + g, [P, NT, HALF]) for g in range(SSM_G)]
    gate_a = cell("gate_a", 5, [P, NT, D])
    gate_b = cell("gate_b", 7, [P, NT, D])
    sum_rows = [cell(f"sum_rows{j}", 9 + 2 * j, [P, HPG, T]) for j in range(2)]
    mix = [cell(f"mix{t}", 13 + t, [P, HPG, P]) for t in range(NT)]
    yaT_hi = cell("yaT_hi", 15, [P, KD, T], F32R)
    yaT_lo = cell("yaT_lo", 17, [P, KD, T], F32R)
    mT_hi = cell("mT_hi", 15, [P, KD, T], F32R)
    mT_lo = cell("mT_lo", 17, [P, KD, T], F32R)
    conv_out = cell("conv_out", 19, [P, 4, T])
    cb = cell("cb", 20, [P, NT * SSM_G, P])
    x_end = cell("x_end", 21, [P, HALF])
    y_off = cell("y_off", 21, [P, HALF], plus=2048)
    dt_hi = cell("dt_hi", 21, [P, KD, SSM_H], F32R)
    dt_lo = cell("dt_lo", 21, [P, KD, SSM_H], F32R, plus=1024)
    dt_raw = cell("dt_raw", 21, [P, KD, SSM_H], plus=2048)
    s2 = cell("s2", 22, [P, 16, NT * SSM_H])
    dx = cell("dx", 23, [P, NT, HALF])
    sums_T = cell("sums_T", 13, [SSM_H, T])
    y2_cells = [(9, 10), (11, 12), (13, 14), (2, 3)]
    y2_hi = [cell(f"y2_hi{g}", a, [P, 4, T], F32R) for g, (a, b) in enumerate(y2_cells)]
    y2_lo = [cell(f"y2_lo{g}", b, [P, 4, T], F32R) for g, (a, b) in enumerate(y2_cells)]
    (dt_in, dt_abs, dt_, la, a_neg, csum, ctot, e_csum, w_end) = (s2[:, j, :] for j in range(9))
    g_ss = s2[:, 9, :]
    g_r = s2[:, 10, :]
    m_ssm_conv, m_ssm_bias, m_conv_a, ssm_gain, ssm_rows = (
        m2_small[k] for k in ("ssm_conv", "ssm_bias", "conv_a", "ssm_gain", "ssm_rows"))

    M2 = ["B", "C", "x0", "x1", "x2", "x3", "c0", "v0", "b0", "c1", "v1", "b1", "z0", "z1", "z2", "z3",
          "ga0", "ga1", "gb0", "gb1", "oa0", "oa1", "os0", "os1", "mix0", "mix1",
          "k0", "k1", "q0", "q1", "v0x", "v1x"]
    SLOT_OF = {"B": 0, "C": 1, "x0": 0, "x1": 1, "x2": 0, "x3": 1, "c0": 0, "v0": 0, "b0": 1, "c1": 0,
               "v1": 0, "b1": 1, "z0": 0, "z1": 1, "z2": 0, "z3": 1}

    def m2_banks(name):
        return pair((M2.index(name) + 1) % 2)

    READ_BY_VECTOR = ["v0", "v1", "oa0", "oa1", "os0", "os1"]
    READ_BY_SCALAR = [n for n in M2 if n not in READ_BY_VECTOR + ["mix0", "mix1"]]

    def await_read(eng, name):
        if name in READ_BY_VECTOR:
            eng.wait_ge(S["dve_read"], NT * (READ_BY_VECTOR.index(name) + 1))
        else:
            eng.wait_ge(S["act_read"], NT * (READ_BY_SCALAR.index(name) + 1))

    def await_banks(pe, name):
        j = M2.index(name)
        if j >= 2 and M2[j - 2] not in ("mix0", "mix1"):
            await_read(pe, M2[j - 2])

    def m2_loads(sp):
        order = [0, 0, 0, 0, 0, 0]
        for name, tile in (("B", 14), ("C", 15), ("x0", 10), ("x1", 11), ("x2", 12), ("x3", 13),
                           ("c0", 2), ("v0", 4), ("b0", 0), ("c1", 3), ("v1", 5), ("b1", 1),
                           ("z0", 6), ("z1", 7), ("z2", 8), ("z3", 9),
                           ("ga0", 16), ("ga1", 17), ("gb0", 18), ("gb1", 19)):
            for i in range(2):
                load(sp, units["m2." + name], i, w["t_m2_in"][tile])
        for half in range(2):
            for i in range(2):
                load(sp, units[f"m2.oa{half}"], i, w["t_m2_oa"][half])
        for half in range(2):
            for j in range(2):
                for i in range(2):
                    load(sp, units[f"m2.os{half}.{j}"], i, w["t_m2_os"][half])
        for name in ("mix_a", "mix_b"):
            for i in range(2):
                load(sp, units["m2." + name], i, w["t_m2_mix"][i])
        for name, what, tile in (("k0", "kv", 0), ("k1", "kv", 1), ("q0", "q", 0), ("q1", "q", 1),
                                 ("v0", "kv", 2), ("v1", "kv", 3)):
            for i in range(2):
                load(sp, units["xa." + name], i, w["t_xa_" + what][tile])
        for name in ("o_a", "o_b"):
            for i in range(2):
                load(sp, units["xa." + name], i, w["t_xa_o"][i])

    def heads_over(v, n, width):
        return v.rearrange("p (h a) -> p h a", a=1).broadcast_to([P, n, width])

    def m2_tensor(pe):
        at = {}

        def run(name):
            u = units["m2." + name]
            await_banks(pe, name)
            for i in range(2):
                sides = {k: at[(name, i, k)] for k in range(4) if (name, i, k) in at}
                if name == "B":
                    pe.wait_ge(xlo_done, 2 * B_MIX2 + i + 1)
                multiply(pe, u, i, xT_hi, xT_lo, m2_banks(name), i == 0, i == 1, None, sides)

        def features(name, slot, before, signal):
            def go():
                await_read(pe, name)
                for b in before:
                    pe.wait_ge(S[b[0]], b[1])
                to_features(pe, proj[:, slot, :, :], 0).then_inc(S[signal], 1)
            return go

        def B_tokens():
            pe.wait_ge(S["B_act"], 4)
            for g in range(SSM_G):
                tr = pe.transpose(work[:, 2, g * P:(g + 1) * P], B_feat[:, g, 0:P], ident[:, :])
            tr.then_inc(step("B_tok_t"), 1)

        def decay_sums():
            pe.wait_ge(*once("la_ready"))
            pe.matmul(work[:, 3, 0:64], up_to[:, :], la, start=True, stop=True)
            mm = pe.matmul(work[:, 3, 64:128], ones[:, :], la, start=True, stop=True)
            for t in range(NT):
                mm = pe.matmul(work[0:SSM_H, 3, P + t * P:P + (t + 1) * P], la[:, t * SSM_H:(t + 1) * SSM_H],
                               up_to[:, :], start=True, stop=True)
            mm.then_inc(step("dt_sums"), 1)

        def cb_products():
            pe.wait_ge(S["C_act"], 4)
            pe.wait_ge(*once("B_tok_ready"))
            pe.wait_ge(S["dt_sums_read"], 2)
            for t in range(NT):
                tok = slice(t * P, (t + 1) * P)
                for g in range(SSM_G):
                    mm = pe.matmul(work[:, 2 + t, g * P:(g + 1) * P], B_feat[:, g, tok], C_feat[:, g, tok],
                                   start=True, stop=True)
            mm.then_inc(step("cb_done"), 1)

        def x_tokens(g):
            def go():
                pe.wait_ge(S["x_act"], 4 * (g + 1))
                if 0 < g < 3:
                    pe.wait_ge(S["x_tok_read"], 2 * g)
                elif g == 0:
                    pe.wait_ge(S["cb_ready"], NT)
                to_tokens(pe, conv_out, 2 if g < 3 else 0).then_inc(S["x_tok_t"], 1)
            return go

        def y_head(g, t):
            for h in range(HPG):
                c = slice(h * SSM_HD, (h + 1) * SSM_HD)
                mm = pe.matmul(work[:, 2, c], mix[t][:, h, :], x_tok[g][:, t, c], start=True, stop=True)
            return mm

        def group_a(g):
            def go():
                if g == 0:
                    pe.wait_ge(S["x_tok_read"], 6)
                else:
                    pe.wait_ge(S["y_ready"], 2 * g)
                pe.wait_ge(S["x_end_ready"], g + 1)
                pe.matmul(work[:, 3, :], B_tok0[:, g * P:(g + 1) * P], x_end[:, :], start=True,
                          stop=True).then_inc(S["state_done"], 1)
                pe.wait_ge(S["mix_ready"], 2 * g + 1)
                y_head(g, 0).then_inc(S["y_diag"], 1)
            return go

        def group_bc(g):
            def go():
                pe.wait_ge(S["state0_ready"], g + 1)
                pe.matmul(work[:, 3, :], C_feat[:, g, P:T], state0[:, :], start=True,
                          stop=True).then_inc(S["y_off_done"], 1)
                pe.wait_ge(S["mix_ready"], 2 * g + 2)
                pe.wait_ge(S["y_ready"], 2 * g + 1)
                y_head(g, 1).then_inc(S["y_diag"], 1)
            return go

        def y_features(g):
            def go():
                pe.wait_ge(S["y_scaled"], NT * (g + 1))
                if g == 0:
                    pe.wait_ge(S["ya_parts"], 2)
                else:
                    pe.wait_ge(S["y2_split"], 4 * g)
                to_features(pe, x_tok[g], 0).then_inc(S["y_t"], 1)
            return go

        at[("B", 0, 1)] = lambda: transpose_x(pe, B_MIX2, 1)
        at[("C", 0, 1)] = features("B", 0, [], "feat_t")
        at[("x0", 0, 1)] = features("C", 1, [("ssm_conv", 1)], "feat_t")
        at[("x0", 0, 2)] = B_tokens
        at[("x0", 0, 3)] = decay_sums
        at[("x1", 0, 0)] = cb_products
        at[("x1", 0, 1)] = features("x0", 0, [("ssm_conv", 2)], "feat_t")
        for g, name in enumerate(("x2", "x3", "c0", "v0")):
            at[(name, 0, 0)] = x_tokens(g)
            if g < 3:
                at[(name, 0, 1)] = features(f"x{g + 1}", (g + 1) % 2, [("ssm_conv", 3 + g)], "feat_t")
        for g, (first, second) in enumerate(((("b0", 0, 0), ("b0", 0, 2)), (("c1", 0, 3), ("c1", 1, 1)),
                                             (("b1", 0, 0), ("b1", 0, 2)), (("z0", 0, 3), ("z0", 1, 1)))):
            at[first] = group_a(g)
            at[second] = group_bc(g)
        at[("b0", 1, 1)] = features("v0", 0, [("x_tok_read", 8)], "cv_t")
        at[("v1", 0, 1)] = features("b0", 1, [("a_conv", 1)], "b_t")
        at[("b1", 1, 1)] = features("v1", 0, [("ya_parts", 1)], "cv_t")
        at[("z0", 1, 0)] = features("b1", 1, [("a_conv", 2)], "b_t")
        for g, name in enumerate(("z2", "z3", "ga0", "ga1")):
            at[(name, 0, 1)] = y_features(g)

        run("B")
        pe.wait_ge(*once("dt_split"))
        narrow(pe, dt_hi, dt_lo, SSM_H, lambda t: work[:, 3, SSM_H * t:SSM_H * (t + 1)]).then_inc(step("dt_done"), 1)
        for name in M2[1:20]:
            run(name)
        for half in range(2):
            await_banks(pe, f"oa{half}")
            pe.wait_ge(S["ya_parts"], 2)
            for i in range(2):
                multiply(pe, units[f"m2.oa{half}"], i, yaT_hi, yaT_lo, m2_banks(f"oa{half}"), i == 0, i == 1)

        def m_features(half):
            pe.wait_ge(S["merged"], NT * (half + 1))
            if half:
                pe.wait_ge(S["m_split"], 2)
            else:
                pe.wait_ge(S["y2_split"], 16)
            for blk in range(4):
                c = half * HALF + blk * P
                for t in range(NT):
                    tr = pe.transpose(work[:, blk // 2, (blk % 2) * T + t * P:(blk % 2) * T + (t + 1) * P],
                                      gate_a[:, t, c:c + P], ident[:, :])
            tr.then_inc(S["m_t"], 1)

        for half in range(2):
            await_banks(pe, f"os{half}")
            for j in range(2):
                for i in range(2):
                    g = 2 * j + i
                    pe.wait_ge(S["y2_split"], 4 * (g + 1))
                    sides = {3: lambda: m_features(0)} if half == 1 and g == 0 else None
                    multiply(pe, units[f"m2.os{half}.{j}"], i, y2_hi[g], y2_lo[g], m2_banks(f"os{half}"),
                             g == 0, g == 3, None, sides, k0=4 * g)
        a, b = units["m2.mix_a"], units["m2.mix_b"]
        pe.wait_ge(S["m_split"], 2)
        for half in range(2):
            await_banks(pe, f"mix{half}")
            sides = {3: lambda: m_features(1)} if half == 0 else None
            multiply(pe, a, half, mT_hi, mT_lo, m2_banks(f"mix{half}"), True, False, None, sides)
        def mem_features(half):
            pe.wait_ge(S["mem_loaded"], 16)
            if half:
                pe.wait_ge(S["mem_split"], 4)
            else:
                pe.wait_ge(S["m_split"], 4)
            for blk in range(4):
                c = half * HALF + blk * P
                for t in range(NT):
                    tr = pe.transpose(work[:, blk // 2, (blk % 2) * T + t * P:(blk % 2) * T + (t + 1) * P],
                                      mem[:, t, c:c + P], ident[:, :])
            tr.then_inc(S["mem_t"], 1)

        pe.wait_ge(S["m_split"], 4)
        multiply(pe, b, 0, mT_hi, mT_lo, m2_banks("mix0"), False, True, None, {0: lambda: mem_features(0)})
        multiply(pe, b, 1, mT_hi, mT_lo, m2_banks("mix1"), False, True, None, {1: lambda: mem_features(1)})

    def m2_scalar(act):
        b = B_MIX2

        def evac(name, dst, func=ACT.Copy, scale=None):
            wait_unit_done(act, units["m2." + name])
            for t in range(NT):
                act.activation(dst[:, t, :], m2_banks(name)[t], func,
                               scale=rstd[:, t:t + 1]).then_inc(S["act_read"], 1)

        def split(name, i):
            split_hi(act, units[name], i)

        def act_conv(n, wait_value, dst, first, signal):
            act.wait_ge(S["ssm_conv"], wait_value)
            for blk in range(4):
                act.activation(dst[:, blk, :], conv_out[:, blk, :] , ACT.Silu,
                               bias=m_ssm_bias[:, first + blk:first + blk + 1]).then_inc(S[signal], 1)

        act.dma_start(dt_raw[:, :, :], w["p_dt"]).then_inc(S["dt_loaded"], 16)
        round_xt(act, b, 1)
        act.wait_ge(S["dt_loaded"], 16)
        act.activation(dt_hi[:, :, :], dt_raw[:, :, :], ACT.Copy).then_inc(step("dt_rounded"), 1)
        for t in range(NT):
            alink(act.activation(a_neg[:, t * SSM_H:(t + 1) * SSM_H], ssm_rows[:, 1, :], ACT.Exp))
        await_own(act)
        act.sem_inc(step("a2_ready"), 1)
        split("m2.C", 0)
        split("m2.C", 1)
        act.wait_ge(rstd_ready, b + 1)
        evac("B", proj[:, 0, :, :])
        split("m2.x0", 0)
        act.wait_ge(*once("dt_done"))
        for t in range(NT):
            act.activation(dt_in[:, t * SSM_H:(t + 1) * SSM_H], work[:, 3, t * SSM_H:(t + 1) * SSM_H], ACT.Copy,
                           scale=rstd[:, t:t + 1]).then_inc(S["dt_scaled"], 1)
        act.wait_ge(*once("dt_biased"))
        alink(act.activation(dt_abs, dt_in, ACT.Abs))
        await_own(act)
        alink(act.activation(dt_abs, dt_abs, ACT.Exp, scale=-1.0))
        await_own(act)
        act.activation(dt_abs, dt_abs, ACT.Ln, bias=1.0).then_inc(step("dt_ln"), 1)
        split("m2.x0", 1)
        act_conv(0, 1, B_feat, 16, "B_act")
        evac("C", proj[:, 1, :, :])
        split("m2.x1", 0)
        act.wait_ge(*once("B_tok_t"))
        act.activation(B_tok0[:, :], bank(2), ACT.Copy).then_inc(step("B_tok_ready"), 1)
        act.wait_ge(*once("dt_sums"))
        act.wait_ge(S["dt_sums_read"], 1)
        act.activation(sums_T[:, :], work[0:SSM_H, 3, P:P + T], ACT.Copy).then_inc(S["dt_sums_read"], 1)
        act.wait_ge(S["dt_sums_read"], 2)
        act.dma_start(row_scratch[0:SSM_H, :], sums_T[:, :]).then_inc(S["rows_stored"], 16)
        split("m2.x1", 1)
        act_conv(0, 2, C_feat, 20, "C_act")
        act.wait_ge(S["rows_stored"], 16)
        for g in range(2):
            act.dma_start(sum_rows[g][:, :, :], everywhere(row_scratch[g * HPG:(g + 1) * HPG, :], HPG)
                          ).then_inc(S[f"rows_loaded{g}"], 16)
        for g, (prev, nxt) in enumerate((("x0", "x2"), ("x1", "x3"), ("x2", "c0"), ("x3", "v0"))):
            evac(prev, proj[:, g % 2, :, :])
            split("m2." + nxt, 0)
            if g:
                group_tokens(act, g - 1)
            split("m2." + nxt, 1)
            act_conv(0, 3 + g, conv_out, 4 * g, "x_act")
            if g == 2:
                act.wait_ge(*once("dt_ready"))
                act.wait_ge(*once("w_end_in"))
                act.activation(w_end, w_end, ACT.Exp).then_inc(S["exp_sums"], 1)
                act.activation(e_csum, csum, ACT.Exp).then_inc(S["exp_sums"], 1)
        evac("c0", proj[:, 0, :, :])
        group_tokens(act, 3)
        split("m2.b0", 0)
        decays(act, 0)
        row_loads(act, 2)
        split("m2.b0", 1)
        group_state(act, 0)
        split("m2.c1", 0)
        decays(act, 1)
        row_loads(act, 3)
        split("m2.c1", 1)
        evac("b0", proj[:, 1, :, :])
        split("m2.v1", 0)
        group_state(act, 1)
        split("m2.v1", 1)
        evac("c1", proj[:, 0, :, :])
        decays(act, 2)
        ya_round(act, 0)
        split("m2.b1", 0)
        split("m2.b1", 1)
        group_state(act, 2)
        split("m2.z0", 0)
        decays(act, 3)
        split("m2.z0", 1)
        evac("b1", proj[:, 1, :, :])
        split("m2.z1", 0)
        group_state(act, 3)
        split("m2.z1", 1)
        for g, nxt in enumerate(("z2", "z3", "ga0", "ga1")):
            evac(f"z{g}", proj[:, g % 2, :, :], ACT.Silu)
            if g:
                y2_round(act, g - 1)
            else:
                ya_round(act, 1)
            split("m2." + nxt, 0)
            act.wait_ge(S["y_gated"], NT * (g + 1))
            for t in range(NT):
                square(act, x_tok[g][:, t, :], g_ss[:, NT * g + t:NT * g + t + 1])
            act.wait_ge(squares, squared[0])
            act.sem_inc(S["y_squared"], 1)
            split("m2." + nxt, 1)
            act.wait_ge(S["y_rms"], g + 1)
            for t in range(NT):
                act.activation(x_tok[g][:, t, :], x_tok[g][:, t, :], ACT.Copy,
                               scale=g_r[:, NT * g + t:NT * g + t + 1]).then_inc(S["y_scaled"], 1)
        act.wait_ge(S["y_t"], 4)
        evac("ga0", gate_a[:, :, 0:HALF], ACT.Sigmoid)
        y2_round(act, 3)
        split("m2.gb0", 0)
        split("m2.gb0", 1)
        evac("ga1", gate_a[:, :, HALF:D], ACT.Sigmoid)
        split("m2.gb1", 0)
        split("m2.gb1", 1)
        evac("gb0", gate_b[:, :, 0:HALF], ACT.Sigmoid)
        split("m2.oa0", 0)
        split("m2.oa0", 1)
        evac("gb1", gate_b[:, :, HALF:D], ACT.Sigmoid)
        split("m2.oa1", 0)
        split("m2.oa1", 1)
        act.wait_ge(S["ya_parts"], 2)
        act.dma_start(mem[:, :, :], w["mem"][0].rearrange("(t p) d -> p t d", p=P)).then_inc(S["mem_loaded"], 16)
        split("m2.os0.0", 0)
        split("m2.os0.0", 1)
        split("m2.os0.1", 0)
        split("m2.os0.1", 1)
        act.wait_ge(S["mem_loaded"], 16)
        for half in range(2):
            for t in range(NT):
                square(act, mem[:, t, half * HALF:(half + 1) * HALF], mem_ss[:, 2 * t + half:2 * t + half + 1])
        act.wait_ge(squares, squared[0])
        act.sem_inc(step("mem_squared"), 1)
        split("m2.os1.0", 0)
        split("m2.os1.0", 1)
        split("m2.os1.1", 0)
        m_round(act, 0)
        split("m2.os1.1", 1)
        split("m2.mix_a", 0)
        split("m2.mix_a", 1)
        split("m2.mix_b", 0)
        m_round(act, 1)
        split("m2.mix_b", 1)
        mem_round(act, 0)
        split("xa.k0", 0)
        square_x(act, B_XA, 0)
        mem_round(act, 1)
        split("xa.k0", 1)
        square_x(act, B_XA, 1)

    def group_tokens(act, g):
        act.wait_ge(S["x_tok_t"], g + 1)
        for t in range(NT):
            act.activation(x_tok[g][:, t, :], bank((2 if g < 3 else 0) + t),
                           ACT.Copy).then_inc(S["x_tok_read"], 1)

    def decays(act, g):
        for t in range(NT):
            act.wait_ge(S["diff2"], 2 * g + t + 1)
            act.activation(flat(mix[t]), flat(mix[t]), ACT.Exp).then_inc(S["decay2"], 1)

    def group_state(act, g):
        act.wait_ge(S["state_done"], g + 1)
        act.activation(state0[:, :], bank(3), ACT.Copy).then_inc(S["state0_ready"], 1)

    def ya_round(act, half):
        act.wait_ge(S["ya_made"], half + 1)
        act.activation(flat(yaT_hi[:, 4 * half:4 * half + 4, :]), flat(conv_out), ACT.Copy).then_inc(S["ya_rounded2"], 1)

    def y2_round(act, g):
        act.wait_ge(S["y_t"], g + 1)
        for blk in range(4):
            act.activation(y2_hi[g][:, blk, :], feature_block(0, blk), ACT.Copy,
                           scale=ssm_gain[:, 4 * g + blk:4 * g + blk + 1]).then_inc(S["y2_rounded"], 1)

    def m_round(act, half):
        act.wait_ge(S["m_t"], half + 1)
        for j in range(2):
            act.activation(flat(mT_hi[:, 4 * half + 2 * j:4 * half + 2 * j + 2, :]), bank(j),
                           ACT.Copy).then_inc(S["m_rounded"], 1)

    def mem_round(act, half):
        act.wait_ge(S["mem_t"], half + 1)
        for k in range(4):
            act.activation(memT_hi[:, 4 * half + k, :], feature_block(0, k), ACT.Copy,
                           scale=mem_gain[:, 4 * half + k:4 * half + k + 1]).then_inc(S["mem_rounded"], 1)

    def m2_vector(dve):
        wt = lambda first: (lambda blk, tap: m_ssm_conv[:, first + blk, tap:tap + 1])
        per_head = "p (h c) -> p h c"

        def ssm_conv(j, first):
            dve.wait_ge(S["feat_t"], j + 1)
            if j == 1:
                dve.wait_ge(S["B_act"], 4)
            elif j == 2:
                dve.wait_ge(S["C_act"], 4)
            elif j > 2:
                dve.wait_ge(S["x_tok_t"], j - 2)
            conv(dve, 0, conv_out, SSM_CONV_K, wt(first))
            dwait(dve)
            dve.sem_inc(S["ssm_conv"], 1)

        def split(name):
            split_lo(dve, units[name], 0)

        rest_xt(dve, B_MIX2, 1)
        dve.wait_ge(*once("dt_rounded"))
        dve.tensor_tensor(dt_lo[:, :, :], dt_raw[:, :, :], dt_hi[:, :, :].bitcast(F32),
                          ALU.subtract).then_inc(step("dt_split"), 1)
        split("m2.C")
        dve.wait_ge(S["dt_scaled"], NT)
        for t in range(NT):
            c = slice(t * SSM_H, (t + 1) * SSM_H)
            dlink(dve.tensor_tensor(dt_in[:, c], dt_in[:, c], ssm_rows[:, 0, :], ALU.add))
        dwait(dve)
        dve.sem_inc(step("dt_biased"), 1)
        split("m2.x0")
        ssm_conv(0, 16)
        dve.wait_ge(*once("dt_ln"))
        dlink(dve.scalar_tensor_tensor(out=dt_, in0=dt_in, scalar=0.0, in1=dt_abs, op0=ALU.max, op1=ALU.add))
        dwait(dve)
        dve.wait_ge(*once("a2_ready"))
        dve.scalar_tensor_tensor(out=la, in0=dt_, scalar=-1.0, in1=a_neg, op0=ALU.mult,
                                 op1=ALU.mult).then_inc(step("la_ready"), 1)
        split("m2.x1")
        dve.wait_ge(*once("dt_sums"))
        dlink(dve.tensor_copy(csum, work[:, 3, 0:64]))
        dlink(dve.tensor_copy(ctot, work[:, 3, 64:128]))
        dwait(dve)
        dve.sem_inc(S["dt_sums_read"], 1)
        dlink(dve.tensor_tensor(w_end, ctot, csum, ALU.subtract))
        dwait(dve)
        dve.sem_inc(step("w_end_in"), 1)
        dve.sem_inc(step("dt_ready"), 1)
        ssm_conv(1, 20)
        split("m2.x2")
        dve.wait_ge(*once("cb_done"))
        tri = up_to[:, :].rearrange("p (a b) -> p a b", a=1).broadcast_to([P, SSM_G, P])
        for t in range(NT):
            dve.tensor_tensor(cb[:, SSM_G * t:SSM_G * (t + 1), :], work[:, 2 + t, :].rearrange(per_head, h=SSM_G),
                              tri, ALU.mult).then_inc(S["cb_ready"], 1)
        ssm_conv(2, 0)
        split("m2.x3")
        ssm_conv(3, 4)
        split("m2.c0")
        ssm_conv(4, 8)
        dve.wait_ge(S["exp_sums"], 2)
        dlink(dve.tensor_tensor(w_end, w_end, dt_, ALU.mult))
        dwait(dve)
        dve.sem_inc(step("w_end_ready"), 1)
        split("m2.v0")
        ssm_conv(5, 12)
        differences(dve, 0, 0)
        differences(dve, 0, 1)
        split("m2.b0")
        mixes(dve, 0)
        outputs_and_differences(dve, 0)
        wait_unit_done(dve, units["m2.v0"])
        await_read(dve, "c0")
        for t in range(NT):
            dve.scalar_tensor_tensor(out=proj[:, 0, t, :], in0=m2_banks("v0")[t], scalar=rstd[:, t:t + 1],
                                     in1=proj[:, 0, t, :], op0=ALU.mult, op1=ALU.mult).then_inc(S["dve_read"], 1)
        split("m2.c1")
        conv_a(dve, 0)
        mixes(dve, 1)
        split("m2.v1")
        outputs_and_differences(dve, 1)
        product_a(dve, 0)
        split("m2.b1")
        mixes(dve, 2)
        outputs_and_differences(dve, 2)
        wait_unit_done(dve, units["m2.v1"])
        await_read(dve, "c1")
        for t in range(NT):
            dve.scalar_tensor_tensor(out=proj[:, 0, t, :], in0=m2_banks("v1")[t], scalar=rstd[:, t:t + 1],
                                     in1=proj[:, 0, t, :], op0=ALU.mult, op1=ALU.mult).then_inc(S["dve_read"], 1)
        split("m2.z0")
        conv_a(dve, 1)
        mixes(dve, 3)
        split("m2.z1")
        outputs_and_differences(dve, 3)
        product_a(dve, 1)
        for g, nxt in enumerate(("z2", "z3", "ga0", "ga1")):
            await_read(dve, f"z{g}")
            dve.wait_ge(S["y_ready"], 2 * (g + 1))
            for t in range(NT):
                dve.tensor_tensor(x_tok[g][:, t, :], x_tok[g][:, t, :], proj[:, g % 2, t, :],
                                  ALU.mult).then_inc(S["y_gated"], 1)
            split("m2." + nxt)
            if g:
                y2_rest(dve, g - 1)
        split("m2.gb0")
        y2_rest(dve, 3)
        for name in ("gb1", "oa0", "oa1", "os0.0"):
            split("m2." + name)
        for half in range(2):
            wait_unit_done(dve, units[f"m2.oa{half}"])
            for t in range(NT):
                c = slice(half * HALF, (half + 1) * HALF)
                if half == 0 and t == 0:
                    await_read(dve, "ga0")
                    await_read(dve, "ga1")
                dve.tensor_tensor(gate_a[:, t, c], gate_a[:, t, c], m2_banks(f"oa{half}")[t],
                                  ALU.mult).then_inc(S["dve_read"], 1)
            split("m2.os0.1" if half == 0 else "m2.os1.0")
        await_read(dve, "gb0")
        await_read(dve, "gb1")
        for half in range(2):
            c = slice(half * HALF, (half + 1) * HALF)
            wait_unit_done(dve, units[f"m2.os{half}.1"])
            await_read(dve, "oa1")
            for t in range(NT):
                dve.tensor_tensor(gate_b[:, t, c], gate_b[:, t, c], m2_banks(f"os{half}")[t],
                                  ALU.mult).then_inc(S["dve_read"], 1)
            await_read(dve, f"os{half}")
            for t in range(NT):
                dve.tensor_tensor(gate_a[:, t, c], gate_a[:, t, c], gate_b[:, t, c],
                                  ALU.add).then_inc(S["merged"], 1)
            split("m2.os1.1" if half == 0 else "m2.mix_b")
            m_rest(dve, half)
            if half == 0:
                split("m2.mix_a")
        mem_rest(dve, 0)
        residual_half(dve, B_XA, 0, units["m2.mix_b"].g + 1, m2_banks("mix0"), 1.0)
        split("xa.k0")
        mem_rest(dve, 1)
        residual_half(dve, B_XA, 1, units["m2.mix_b"].g + 2, m2_banks("mix1"), 1.0)

    def differences(dve, g, t):
        dve.wait_ge(S[f"rows_loaded{g}"], 16)
        if g:
            dve.wait_ge(S["y_diag"], 2 * (g - 1) + t + 1)
        for h in range(HPG):
            n = t * SSM_H + g * HPG + h
            df = dve.tensor_scalar(mix[t][:, h, :], sum_rows[g % 2][:, h, t * P:(t + 1) * P],
                                   csum[:, n:n + 1], 0.0, ALU.subtract, ALU.min)
        df.then_inc(S["diff2"], 1)

    def mixes(dve, g):
        dve.wait_ge(S["cb_ready"], NT)
        for t in range(NT):
            dve.wait_ge(S["decay_dt"], 2 * g + t + 1)
            both = cb[:, SSM_G * t + g:SSM_G * t + g + 1, :].broadcast_to([P, HPG, P])
            dve.tensor_tensor(mix[t][:, :, :], mix[t][:, :, :], both, ALU.mult).then_inc(S["mix_ready"], 1)

    def outputs_and_differences(dve, g):
        per_head = "p (h c) -> p h c"
        dve.wait_ge(S["dx_ready"], g + 1)
        dve.wait_ge(S["y_diag"], 2 * g + 1)
        dve.tensor_tensor(x_tok[g][:, 0, :], bank(2), dx[:, 0, :], ALU.add).then_inc(S["y_ready"], 1)
        if g < SSM_G - 1:
            differences(dve, g + 1, 0)
        dve.wait_ge(S["y_off_done"], g + 1)
        n = SSM_H + g * HPG
        dlink(dve.tensor_tensor(y_off[:, :].rearrange(per_head, h=HPG), bank(3).rearrange(per_head, h=HPG),
                                heads_over(e_csum[:, n:n + HPG], HPG, SSM_HD), ALU.mult))
        dwait(dve)
        dlink(dve.tensor_tensor(y_off[:, :], y_off[:, :], dx[:, 1, :], ALU.add))
        dwait(dve)
        dve.wait_ge(S["y_diag"], 2 * g + 2)
        dve.tensor_tensor(x_tok[g][:, 1, :], bank(2), y_off[:, :], ALU.add).then_inc(S["y_ready"], 1)
        if g < SSM_G - 1:
            differences(dve, g + 1, 1)

    def conv_a(dve, half):
        dve.wait_ge(S["cv_t"], half + 1)
        if half == 0:
            dve.wait_ge(S["x_tok_t"], 4)
        else:
            dve.wait_ge(S["ya_parts"], 1)
        conv(dve, 0, conv_out, CONV_A_K, lambda blk, tap: m_conv_a[:, 4 * half + blk, tap:tap + 1])
        dwait(dve)
        dve.sem_inc(S["a_conv"], 1)

    def product_a(dve, half):
        dve.wait_ge(S["b_t"], half + 1)
        for j in range(2):
            c = conv_out[:, 2 * j:2 * j + 2, :]
            dlink(dve.tensor_tensor(flat(c), flat(c), bank(j), ALU.mult))
        dwait(dve)
        dve.sem_inc(S["ya_made"], 1)
        dve.wait_ge(S["ya_rounded2"], half + 1)
        k = slice(4 * half, 4 * half + 4)
        dve.tensor_tensor(flat(yaT_lo[:, k, :]), flat(conv_out), flat(yaT_hi[:, k, :]).bitcast(F32),
                          ALU.subtract).then_inc(S["ya_parts"], 1)

    def y2_rest(dve, g):
        for blk in range(4):
            if blk % 2 == 0:
                dve.wait_ge(S["y2_rounded"], 4 * g + blk + 2)
            dve.scalar_tensor_tensor(out=y2_lo[g][:, blk, :], in0=feature_block(0, blk),
                                     scalar=ssm_gain[:, 4 * g + blk:4 * g + blk + 1],
                                     in1=y2_hi[g][:, blk, :].bitcast(F32), op0=ALU.mult,
                                     op1=ALU.subtract).then_inc(S["y2_split"], 1)

    def m_rest(dve, half):
        for j in range(2):
            dve.wait_ge(S["m_rounded"], 2 * half + j + 1)
            k = slice(4 * half + 2 * j, 4 * half + 2 * j + 2)
            dve.tensor_tensor(flat(mT_lo[:, k, :]), bank(j), flat(mT_hi[:, k, :]).bitcast(F32),
                              ALU.subtract).then_inc(S["m_split"], 1)

    def mem_rest(dve, half):
        for k in range(4):
            if k % 2 == 0:
                dve.wait_ge(S["mem_rounded"], 4 * half + k + 2)
            dve.scalar_tensor_tensor(out=memT_lo[:, 4 * half + k, :], in0=feature_block(0, k),
                                     scalar=mem_gain[:, 4 * half + k:4 * half + k + 1],
                                     in1=memT_hi[:, 4 * half + k, :].bitcast(F32), op0=ALU.mult,
                                     op1=ALU.subtract).then_inc(S["mem_split"], 1)

    def m2_pool(pool):
        per_head = "p (h c) -> p h c"

        def split(name):
            split_lo(pool, units[name], 1)

        def group(g):
            n = g * HPG
            if g:
                pool.wait_ge(S["state_done"], g)
                pool.wait_ge(S["y_ready"], 2 * g)
            pool.wait_ge(S["x_tok_read"], 2 * (g + 1))
            pool.wait_ge(*once("w_end_ready"))
            pool.tensor_tensor(x_end[:, :].rearrange(per_head, h=HPG), x_tok[g][:, 0, :].rearrange(per_head, h=HPG),
                               heads_over(w_end[:, n:n + HPG], HPG, SSM_HD), ALU.mult).then_inc(S["x_end_ready"], 1)
            for t in range(NT):
                plink(pool.tensor_tensor(dx[:, t, :].rearrange(per_head, h=HPG),
                                         x_tok[g][:, t, :].rearrange(per_head, h=HPG),
                                         heads_over(ssm_rows[:, 2, n:n + HPG], HPG, SSM_HD), ALU.mult))
            pwait(pool)
            pool.sem_inc(S["dx_ready"], 1)
            for t in range(NT):
                pool.wait_ge(S["decay2"], 2 * g + t + 1)
                pool.tensor_tensor(mix[t][:, :, :], mix[t][:, :, :],
                                   heads_over(dt_[:, t * SSM_H + n:t * SSM_H + n + HPG], HPG, P),
                                   ALU.mult).then_inc(S["decay_dt"], 1)

        for name in ("C", "x0", "x1", "x2", "x3", "c0", "v0"):
            split("m2." + name)
        for g, names in enumerate((("b0",), ("c1", "v1"), ("b1",), ("z0", "z1"))):
            group(g)
            for name in names:
                split("m2." + name)
        for g, name in enumerate(("z2", "z3", "ga0", "ga1")):
            split("m2." + name)
            pool.wait_ge(S["y_squared"], g + 1)
            c = slice(NT * g, NT * (g + 1))
            plink(pool.tensor_scalar(g_r[:, c], g_ss[:, c], 1.0 / HALF, EPS, ALU.mult, ALU.add))
            pwait(pool)
            plink(pool.tensor_tensor(g_r[:, c], g_r[:, c], minus_half[:, 0:NT], ALU.pow))
            pwait(pool)
            pool.sem_inc(S["y_rms"], 1)
        for name in ("gb0", "gb1", "oa0", "oa1", "os0.0", "os0.1", "os1.0", "os1.1", "mix_a", "mix_b"):
            split("m2." + name)
        pool.wait_ge(*once("mem_squared"))
        pairs = mem_ss.rearrange("p (t a) -> p t a", t=NT)
        plink(pool.tensor_tensor(mem_r, pairs[:, :, 0], pairs[:, :, 1], ALU.add))
        pwait(pool)
        plink(pool.tensor_scalar(mem_r, mem_r, 1.0 / D, EPS, ALU.mult, ALU.add))
        pwait(pool)
        pool.tensor_tensor(mem_r, mem_r, minus_half[:, 0:NT], ALU.pow).then_inc(S["mem_rms"], 1)
        split("xa.k0")
        reciprocal_rms(pool, B_XA)

    def row_loads(act, g):
        act.wait_ge(S["diff2"], 2 * (g - 1))
        act.dma_start(sum_rows[g % 2][:, :, :], everywhere(row_scratch[g * HPG:(g + 1) * HPG, :], HPG)
                      ).then_inc(S[f"rows_loaded{g}"], 16)

    memT_hi = cell("memT_hi", 9, [P, KD, T], F32R)
    memT_lo = cell("memT_lo", 11, [P, KD, T], F32R)
    mem = cell("mem", 19, [P, NT, D])
    key_feat = cell("key_feat", 2, [P, KD, T])
    value = cell("value", 4, [P, NT, D])
    query_feat = cell("query_feat", 6, [P, KD, T])
    probs = cell("probs", 13, [P, 2, NT, 512])
    probs_T = cell("probs_T", 15, [P, 2, 4, T])
    attn = cell("attn", 17, [P, NT, D])
    attnT_hi = cell("attnT_hi", 9, [P, KD, T], F32R)
    attnT_lo = cell("attnT_lo", 11, [P, KD, T], F32R)
    xs_small = cell("xs_small", 21, [P, 8, 16])
    row_max, minus_max, row_sum, inv_sum = (xs_small[:, j, :] for j in range(4))
    SCALE = XDH ** -0.5

    def xa_tensor(pe):
        def run(unit, name, xhi, xlo, at, waits=(None, None)):
            await_banks(pe, name)
            for i in range(2):
                if waits[i]:
                    pe.wait_ge(*waits[i])
                multiply(pe, units["xa." + unit], i, xhi, xlo, m2_banks(name), i == 0, i == 1, None,
                         {k: at[(i, k)] for k in range(4) if (i, k) in at})

        def rows_features(name, slot, before, signal):
            def go():
                await_read(pe, name)
                for s, v in before:
                    pe.wait_ge(S[s], v)
                to_features(pe, proj[:, slot, :, :], 0).then_inc(S[signal], 1)
            return go

        def scores(hp):
            def go():
                pe.wait_ge(S["query_feat_ready"], 2 * (hp + 1))
                pe.wait_ge(S["key_feat_ready"], 4)
                if hp:
                    pe.wait_ge(S["probs_ready"], 4)
                for t in range(NT):
                    for h in range(2):
                        for k in range(2):
                            kt = 4 * hp + 2 * h + k
                            mm = pe.matmul(work[:, 2 + t, h * MEM:(h + 1) * MEM],
                                           query_feat[:, kt, t * P:(t + 1) * P], key_feat[:, kt, :],
                                           start=k == 0, stop=k == 1)
                mm.then_inc(S["scores2"], 1)
            return go

        def probs_features(hp):
            def go():
                pe.wait_ge(S["probs_ready"], 4 * (hp + 1))
                if hp:
                    pe.wait_ge(S["probs_T_ready"], 2)
                else:
                    pe.wait_ge(S["query_feat_ready"], 4)
                to_features(pe, probs[:, hp, :, :], 0).then_inc(S["probs_t"], 1)
            return go

        def weighted(hp):
            def go():
                pe.wait_ge(S["probs_T_ready"], 2 * (hp + 1))
                await_read(pe, f"v{hp}x")
                pe.wait_ge(S["attn_ready"], 4) if hp else pe.wait_ge(S["probs_ready"], 8)
                for t in range(NT):
                    for h in range(2):
                        for m in range(NT):
                            c = slice((2 * hp + h) * XDH, (2 * hp + h + 1) * XDH)
                            mm = pe.matmul(work[:, 2 + t, h * XDH:(h + 1) * XDH],
                                           probs_T[:, hp, 2 * h + m, t * P:(t + 1) * P], value[:, m, c],
                                           start=m == 0, stop=m == NT - 1)
                mm.then_inc(S["weighted"], 1)
            return go

        def attn_features(hp):
            def go():
                pe.wait_ge(S["attn_ready"], 4 * (hp + 1))
                if hp:
                    pe.wait_ge(S["attn_split"], 2)
                else:
                    pe.wait_ge(S["probs_T_ready"], 4)
                for blk in range(4):
                    c = hp * HALF + blk * P
                    for t in range(NT):
                        tr = pe.transpose(work[:, blk // 2, (blk % 2) * T + t * P:(blk % 2) * T + (t + 1) * P],
                                          attn[:, t, c:c + P], ident[:, :])
                tr.then_inc(S["attn_t"], 1)
            return go

        def x_features(half):
            def go():
                if half == 0:
                    pe.wait_ge(S["mem_split"], 8)
                transpose_x(pe, B_XA, half)
            return go

        def k0_features():
            pe.wait_ge(xlo_done, 2 * B_XA + 1)
            rows_features("k0", 0, [], "k_t")()

        pe.wait_ge(resid_done, 2 * (B_XA - 1) + 1)
        run("k0", "k0", memT_hi, memT_lo, {(0, 3): x_features(0), (1, 1): x_features(1)},
            ((S["mem_split"], 4), (S["mem_split"], 8)))
        pe.wait_ge(resid_done, 2 * (B_XA - 1) + 2)
        run("k1", "k1", memT_hi, memT_lo, {(0, 1): k0_features})
        run("q0", "q0", xT_hi, xT_lo, {(0, 1): rows_features("k1", 1, [("key_feat_ready", 2)], "k_t")},
            ((xlo_done, 2 * B_XA + 1), (xlo_done, 2 * B_XA + 2)))
        run("q1", "q1", xT_hi, xT_lo, {(0, 1): rows_features("q0", 0, [("key_feat_ready", 4)], "q_t"),
                                       (1, 0): scores(0)})
        run("v0", "v0x", memT_hi, memT_lo, {(0, 1): rows_features("q1", 1, [("query_feat_ready", 2)], "q_t"),
                                            (1, 0): scores(1)})
        run("v1", "v1x", memT_hi, memT_lo, {(0, 0): probs_features(0), (0, 3): probs_features(1),
                                            (1, 1): weighted(0), (1, 3): attn_features(0)})
        a, b = units["xa.o_a"], units["xa.o_b"]
        pe.wait_ge(S["attn_split"], 2)
        await_read(pe, "v0x")
        multiply(pe, a, 0, attnT_hi, attnT_lo, pair(1), True, False, None, {2: weighted(1)})
        await_read(pe, "v1x")
        multiply(pe, a, 1, attnT_hi, attnT_lo, pair(0), True, False, None, {1: attn_features(1)})
        pe.wait_ge(S["attn_split"], 4)
        multiply(pe, b, 0, attnT_hi, attnT_lo, pair(1), False, True)
        multiply(pe, b, 1, attnT_hi, attnT_lo, pair(0), False, True, None, {2: lambda: transpose_x(pe, B_FFN3, 0)})

    def xa_scalar(act):
        def split(name, i):
            split_hi(act, units["xa." + name], i)

        def evac(unit, name, dst, scale):
            wait_unit_done(act, units["xa." + unit])
            for t in range(NT):
                act.activation(dst[:, t, :], m2_banks(name)[t], ACT.Copy,
                               scale=scale[:, t:t + 1]).then_inc(S["act_read"], 1)

        def features(signal, n, dst, at, ready):
            act.wait_ge(S[signal], n)
            for j in range(2):
                act.activation(flat(dst[:, at + 2 * j:at + 2 * j + 2, :]), bank(j), ACT.Copy).then_inc(S[ready], 1)

        def softmax(hp):
            act.wait_ge(S["max_ready"], hp + 1)
            for t in range(NT):
                for h in range(2):
                    n = 4 * hp + 2 * t + h
                    act.activation(probs[:, hp, t, h * MEM:(h + 1) * MEM], work[:, 2 + t, h * MEM:(h + 1) * MEM],
                                   ACT.Exp, bias=minus_max[:, n:n + 1], scale=SCALE,
                                   accum_out=row_sum[:, n:n + 1]).then_inc(S["probs_ready"], 1)

        round_xt(act, B_XA, 0)
        split("k1", 0)
        split("k1", 1)
        act.wait_ge(S["mem_rms"], 1)
        evac("k0", "k0", proj[:, 0, :, :], mem_r)
        split("q0", 0)
        features("k_t", 1, key_feat, 0, "key_feat_ready")
        round_xt(act, B_XA, 1)
        split("q0", 1)
        evac("k1", "k1", proj[:, 1, :, :], mem_r)
        split("q1", 0)
        features("k_t", 2, key_feat, 4, "key_feat_ready")
        split("q1", 1)
        act.wait_ge(rstd_ready, B_XA + 1)
        evac("q0", "q0", proj[:, 0, :, :], rstd)
        split("v0", 0)
        features("q_t", 1, query_feat, 0, "query_feat_ready")
        split("v0", 1)
        softmax(0)
        evac("q1", "q1", proj[:, 1, :, :], rstd)
        split("v1", 0)
        features("q_t", 2, query_feat, 4, "query_feat_ready")
        split("v1", 1)
        softmax(1)
        evac("v0", "v0x", value[:, :, 0:HALF], mem_r)
        split("o_a", 0)
        features("probs_t", 1, probs_T[:, 0, :, :], 0, "probs_T_ready")
        features("probs_t", 2, probs_T[:, 1, :, :], 0, "probs_T_ready")
        split("o_a", 1)
        attn_scale(act, 0)
        attn_round(act, 0)
        evac("v1", "v1x", value[:, :, HALF:D], mem_r)
        attn_scale(act, 1)
        split("o_b", 0)
        attn_round(act, 1)
        split("o_b", 1)
        u = units["ffn3.up0"]
        split_hi(act, u, 0)
        square_x(act, B_FFN3, 0)
        round_xt(act, B_FFN3, 0)
        split_hi(act, u, 1)
        square_x(act, B_FFN3, 1)
        act.dma_start(gfinal2_row[:, :], w["r_final"][1:2, :].broadcast_to([P, D])).then_inc(S["final_row"], 16)

    def attn_scale(act, hp):
        act.wait_ge(S["weighted"], hp + 1)
        act.wait_ge(S["inv_sum_ready"], hp + 1)
        for t in range(NT):
            for h in range(2):
                n = 4 * hp + 2 * t + h
                c = (2 * hp + h) * XDH
                act.activation(attn[:, t, c:c + XDH], work[:, 2 + t, h * XDH:(h + 1) * XDH], ACT.Copy,
                               scale=inv_sum[:, n:n + 1]).then_inc(S["attn_ready"], 1)

    def attn_round(act, hp):
        act.wait_ge(S["attn_t"], hp + 1)
        for j in range(2):
            act.activation(flat(attnT_hi[:, 4 * hp + 2 * j:4 * hp + 2 * j + 2, :]), bank(j),
                           ACT.Copy).then_inc(S["attn_rounded"], 1)

    def xa_vector(dve):
        def split(name):
            split_lo(dve, units["xa." + name], 0)

        def maxima(hp):
            dve.wait_ge(S["scores2"], hp + 1)
            n = slice(4 * hp, 4 * hp + 4)
            for t in range(NT):
                dlink(dve.tensor_reduce(row_max[:, 4 * hp + 2 * t:4 * hp + 2 * t + 2],
                                        work[:, 2 + t, :].rearrange("p (h m) -> p h m", h=2),
                                        mybir.AxisListType.X, ALU.max))
            dwait(dve)
            dlink(dve.tensor_scalar(minus_max[:, n], row_max[:, n], -SCALE, None, ALU.mult))
            dwait(dve)
            dve.sem_inc(S["max_ready"], 1)

        def sums(hp):
            dve.wait_ge(S["probs_ready"], 4 * (hp + 1))
            n = slice(4 * hp, 4 * hp + 4)
            dve.reciprocal(inv_sum[:, n], row_sum[:, n]).then_inc(S["inv_sum_ready"], 1)

        def rest(hp):
            for j in range(2):
                dve.wait_ge(S["attn_rounded"], 2 * hp + j + 1)
                k = slice(4 * hp + 2 * j, 4 * hp + 2 * j + 2)
                dve.tensor_tensor(flat(attnT_lo[:, k, :]), bank(j), flat(attnT_hi[:, k, :]).bitcast(F32),
                                  ALU.subtract).then_inc(S["attn_split"], 1)

        rest_xt(dve, B_XA, 0)
        split("k1")
        split("q0")
        rest_xt(dve, B_XA, 1)
        split("q1")
        split("v0")
        maxima(0)
        sums(0)
        split("v1")
        maxima(1)
        sums(1)
        split("o_a")
        rest(0)
        split("o_b")
        rest(1)
        residual_half(dve, B_FFN3, 0, units["xa.o_b"].g + 1, pair(1), 1.0)
        split_lo(dve, units["ffn3.up0"], 0)
        rest_xt(dve, B_FFN3, 0)
        residual_half(dve, B_FFN3, 1, units["xa.o_b"].g + 2, pair(0), 1.0)

    def xa_pool(pool):
        for name in ("k1", "q0", "q1", "v0", "v1", "o_a", "o_b"):
            split_lo(pool, units["xa." + name], 1)
        split_lo(pool, units["ffn3.up0"], 1)
        reciprocal_rms(pool, B_FFN3)

    CONSTS = [(ident[:, :], w["c_ident"]), (up_to[:, :], w["c_up_to"]), (below[:, :], w["c_below"]),
              (level_mask[:, :, :], w["c_levels"])]
    N_CONSTS = len(CONSTS)

    def everywhere(a, n):
        return a.rearrange("(o a) h -> o a h", o=1).broadcast_to([P, n, a.shape[-1]])

    PARAMS = [(ba_raw[:, :, :], w["p_ba"]), (m1_conv[:, :, :], w["p_m1_conv"]),
              (gm_bias[:, :], w["p_gm_bias"]), (gm_wT[:, :, :], w["p_gm_wT"]), (dn_gain[:, :], w["p_dn_gain"]),
              (gm_rows[:, :, :], everywhere(w["r_gm"], 2)), (dn_rows[:, :, :], everywhere(w["r_dn"], 2)),
              (m_ssm_conv[:, :, :], w["p_ssm_conv"]), (m_ssm_bias[:, :], w["p_ssm_bias"]),
              (m_conv_a[:, :, :], w["p_conv_a"]), (ssm_gain[:, :], w["p_ssm_gain"]),
              (ssm_rows[:, :, :], everywhere(w["r_ssm"], 3)), (mem_gain[:, :], w["p_mem_gain"])]

    def start_scalar(act):
        act.dma_start(gain[:, :, :], w["p_gains"]).then_inc(S["gains_loaded"], 16)
        for dst, src in PARAMS:
            act.dma_start(dst, src).then_inc(params_loaded, 16)
        u0 = units["ffn0.up0"]
        split_hi(act, u0, 0)
        act.wait_ge(S["gains_loaded"], 16)
        round_xt(act, 0, 0)
        split_hi(act, u0, 1)
        square_x(act, 0, 0)
        square_x(act, 0, 1)
        act.wait_ge(params_loaded, 16 * len(PARAMS))

    def start_vector(dve):
        split_lo(dve, units["ffn0.up0"], 0)
        rest_xt(dve, 0, 0)
        dve.wait_ge(params_loaded, 16 * len(PARAMS))
        dve.wait_ge(consts_loaded, 16 * N_CONSTS)
        dve.memset(gm_wT[64:P, :, 0:64], 0.0).then_inc(S["gm_masked"], 1)

    def start_pool(pool):
        pool.memset(ones[:, :], 1.0).then_inc(half_const, 1)
        pool.memset(minus_half[:, :], -0.5).then_inc(half_const, 1)
        pool.wait_ge(half_const, 2)
        split_lo(pool, units["ffn0.up0"], 1)
        reciprocal_rms(pool, 0)

    def finish_vector(dve):
        dve.wait_ge(rstd_ready, B_OUT + 1)
        dve.wait_ge(S["final_row"], 16)
        dve.wait_ge(resid_done, 2 * B_OUT)
        for t in range(NT):
            dve.scalar_tensor_tensor(out=x[:, t, :], in0=x[:, t, :], scalar=rstd[:, t:t + 1], in1=gfinal2_row[:, :],
                                     op0=ALU.mult, op1=ALU.mult).then_inc(fin_done, 1)

    def finish_sync(sp):
        for t in range(NT):
            sp.wait_ge(fin_done, t + 1)
            sp.dma_start(out[0, t * P:(t + 1) * P, :], x[:, t, :]).then_inc(out_stored, 16)
        sp.wait_ge(out_stored, 16 * NT)

    @block.sync
    def _(sp):
        sp.dma_start(x[:, :, :], w["x"][0].rearrange("(t p) d -> p t d", p=P)).then_inc(x_loaded, 16)
        for dst, src in CONSTS:
            sp.dma_start(dst, src).then_inc(consts_loaded, 16)
        ffn_loads(sp, 0)
        m1_loads(sp)
        ffn_loads(sp, 1)
        ffn_loads(sp, 2)
        m2_loads(sp)
        ffn_loads(sp, 3)
        finish_sync(sp)

    @block.scalar
    def _(act):
        start_scalar(act)
        ffn_scalar(act, 0, [units["m1.k"]])
        m1_scalar(act)
        ffn_scalar(act, 1, [units["ffn2.up0"]])
        ffn_scalar(act, 2, [units["m2.B"]])
        m2_scalar(act)
        xa_scalar(act)
        ffn_scalar(act, 3, [])

    @block.vector
    def _(dve):
        start_vector(dve)
        ffn_vector(dve, 0, [units["m1.k"]])
        m1_vector(dve)
        ffn_vector(dve, 1, [units["ffn2.up0"]])
        ffn_vector(dve, 2, [units["m2.B"]])
        m2_vector(dve)
        xa_vector(dve)
        ffn_vector(dve, 3, [])
        finish_vector(dve)

    @block.gpsimd
    def _(pool):
        start_pool(pool)
        ffn_pool(pool, 0, [units["m1.k"]])
        m1_pool(pool)
        ffn_pool(pool, 1, [units["ffn2.up0"]])
        ffn_pool(pool, 2, [units["m2.B"]])
        m2_pool(pool)
        xa_pool(pool)
        ffn_pool(pool, 3, [])

    @block.tensor
    def _(pe):
        transpose_x(pe, 0, 0)
        pe.wait_ge(half_const, 2)
        for f in (0, 1, 2, 3):
            ffn_tensor(pe, f)
            if f == 0:
                m1_tensor(pe)
            elif f == 2:
                m2_tensor(pe)
                xa_tensor(pe)

    ctx.close()




def constants():
    i, j = np.arange(P)[:, None], np.arange(P)[None, :]
    levels = [((i // s) % 2 == 1) & (j // s == i // s - 1) for s in SOLVE_LEVELS]
    return {
        "c_ident": (i == j).astype(np.float32),
        "c_up_to": (i <= j).astype(np.float32),
        "c_below": (i > j).astype(np.float32),
        "c_levels": np.stack(levels + [levels[0].T], axis=1).astype(np.float32),
    }


def by_partition(v):
    return v.reshape(-1, P).T


def tiles(m, n=512):
    K, N = m.shape
    return m.reshape(K // P, P, N // n, n).transpose(2, 1, 0, 3).reshape(N // n, P, K // P * n)


def ffn_up_tiles(gate, up):
    both = np.stack([m.reshape(KD, P, NCH, CH) for m in (gate, up)], axis=3)
    return both.transpose(2, 1, 0, 3, 4).reshape(NCH, P, KD * 2 * CH)


def layout(a):
    out = {"x": a["x"], "mem": a["mem_2"]}
    gate_up = [a["ffn1_w_gate_up_2"][0], a["ffn2_w_gate_up_2"][0]]
    ups = [(a["ffn1_w_gate"][0], a["ffn1_w_up"][0]), (a["ffn2_w_gate"][0], a["ffn2_w_up"][0])]
    ups += [(m[:, :DFF], m[:, DFF:]) for m in gate_up]
    downs = [a[k][0] for k in ("ffn1_w_down", "ffn2_w_down", "ffn1_w_down_2", "ffn2_w_down_2")]
    for f in range(4):
        out[f"t_ffn{f}_up"] = ffn_up_tiles(*ups[f])
        out[f"t_ffn{f}_down"] = tiles(downs[f])
    out["t_m1_in"] = tiles(a["w_in"][0][:, :6 * 512])
    out["t_m1_out"] = tiles(a["w_out"][0])
    out["p_ba"] = a["w_in"][0][:, 6 * 512:].reshape(KD, P, 8).transpose(1, 0, 2)
    out["p_m1_conv"] = a["dn_conv_w"][0].reshape(TAPS1, 12, P).transpose(2, 1, 0)
    out["p_gm_bias"] = a["gm_b_s"][0].T
    out["p_gm_wT"] = a["gm_w_s"][0].transpose(2, 0, 1)
    out["p_dn_gain"] = by_partition(a["dn_norm"][0])
    out["r_gm"] = np.stack([a["gm_ln_g"][0], a["gm_ln_b"][0]])
    out["r_dn"] = np.stack([a["dn_dt_bias"][0], a["dn_a_log"][0]])
    out["r_final"] = np.stack([a["final_norm"], a["final_norm_2"]])
    norms = ("ffn1_norm", "mix_norm", "ffn2_norm", "ffn1_norm_2", "mix_norm_2", "xattn_norm_2", "ffn2_norm_2")
    w_in = a["w_in_2"][0]
    dt_at = 3 * D + 2 * SSM_IN + 2 * SSM_G * SSM_N
    out["t_m2_in"] = np.concatenate([tiles(w_in[:, :dt_at]), tiles(w_in[:, dt_at + SSM_H:])])
    out["p_dt"] = w_in[:, dt_at:dt_at + SSM_H].reshape(KD, P, SSM_H).transpose(1, 0, 2)
    for name, key in (("t_m2_oa", "w_out_a_2"), ("t_m2_os", "w_out_ssm_2"), ("t_m2_mix", "w_mix_out_2"),
                      ("t_xa_kv", "w_kv_2"), ("t_xa_q", "w_q_2"), ("t_xa_o", "w_o_x_2")):
        out[name] = tiles(a[key][0])
    out["p_ssm_conv"] = a["ssm_conv_w_2"][0].reshape(SSM_CONV_K, 24, P).transpose(2, 1, 0)
    out["p_ssm_bias"] = by_partition(a["ssm_conv_b_2"][0])
    out["p_conv_a"] = a["conv_a_w_2"][0].reshape(CONV_A_K, KD, P).transpose(2, 1, 0)
    out["p_ssm_gain"] = by_partition(a["ssm_norm_2"][0])
    out["p_mem_gain"] = by_partition(a["mem_norm_2"][0])
    out["r_ssm"] = np.stack([a["ssm_dt_bias_2"][0], a["ssm_a_log_2"][0], a["ssm_d_2"][0]])
    out["p_gains"] = np.stack([by_partition(a[k][0]) for k in norms], axis=1)
    return out


def kernel(**inputs):
    import concourse.bacc as bacc
    from concourse.bass_utils import run_bass_kernel_spmd

    nc = bacc.Bacc("TRN2", target_bir_lowering=False, num_devices=1, dynamic_dma_scratch_size=1024)
    arrays, aps = {}, {}
    for name, a in {**layout(inputs), **constants()}.items():
        a = np.ascontiguousarray(a)
        arrays[f"in_{name}"] = a
        aps[name] = nc.dram_tensor(f"in_{name}", a.shape, mybir.dt.from_np(a.dtype), kind="ExternalInput").ap()
    out = nc.dram_tensor("out", (1, T, D), F32, kind="ExternalOutput").ap()
    rows = nc.dram_tensor("row_scratch", (64, T), F32, kind="Internal").ap()
    build(nc, aps, out, rows)
    r = run_bass_kernel_spmd(nc, [arrays], core_ids=[0])
    return r.results[0]["out"]
```
